# Optimizing a Trainium2 kernel written in Bass

```python
import math
import jax, jax.numpy as jnp
from jax import lax
import numpy as np

D_MODEL = 1024
BATCH = 1
SEQ = 1024
DEPTH = 1

N_MIXERS = 3
CHUNK = 64
Q_BLOCK = 128
RMS_EPS = 1e-6
LN_EPS = 1e-5
CONV_WIDTH = D_MODEL
CONV_K = 31
FOX_HEAD_DIM = 64
FOX_HEADS = D_MODEL // FOX_HEAD_DIM
FOX_WIDTH = FOX_HEADS * FOX_HEAD_DIM
SSM_WIDTH = D_MODEL
SSM_GROUP = 16
SSM_GROUPS = SSM_WIDTH // SSM_GROUP
SSM_STATE = 64
DT_MIN = 1e-3
DT_MAX = 1e-1

N_CONV_LAYERS = len(range(0, DEPTH, N_MIXERS))
N_FOX_LAYERS = len(range(1, DEPTH, N_MIXERS))
N_SSM_LAYERS = len(range(2, DEPTH, N_MIXERS))

kernel_name = "interleaved_conv_fox_s5_trunk"

def rms_norm(x, g):
    xf = x.astype(jnp.float32)
    y = xf * lax.rsqrt(jnp.mean(xf * xf, axis=-1, keepdims=True) + RMS_EPS)
    return (y * g.astype(jnp.float32)).astype(x.dtype)

def head_rms(x, g):
    xf = x.astype(jnp.float32)
    return xf * lax.rsqrt(jnp.mean(xf * xf, axis=-1, keepdims=True) + RMS_EPS) * g.astype(jnp.float32)

def conv_mixer(h, w_in, conv_w, conv_b, ln_g, ln_b, w_out):
    z = h @ w_in
    a, b, gate = jnp.split(z, 3, axis=-1)
    u = a * jax.nn.sigmoid(b)
    u = lax.conv_general_dilated(
        u, conv_w[:, None, :], window_strides=(1,), padding=[(CONV_K - 1, 0)],
        dimension_numbers=("NWC", "WIO", "NWC"), feature_group_count=CONV_WIDTH,
    ) + conv_b
    uf = u.astype(jnp.float32)
    mu = jnp.mean(uf, axis=-1, keepdims=True)
    var = jnp.mean(jnp.square(uf - mu), axis=-1, keepdims=True)
    uf = (uf - mu) * lax.rsqrt(var + LN_EPS) * ln_g.astype(jnp.float32) + ln_b.astype(jnp.float32)
    u = jax.nn.silu(uf).astype(h.dtype) * jax.nn.silu(gate)
    return u @ w_out

def fox_mixer(h, w_in, f_bias, q_g, k_g, w_out):
    bsz, seq, _ = h.shape
    z = h @ w_in
    q, k, v, gate, f_logit = jnp.split(
        z, [FOX_WIDTH, 2 * FOX_WIDTH, 3 * FOX_WIDTH, 4 * FOX_WIDTH], axis=-1)
    shp = (bsz, seq, FOX_HEADS, FOX_HEAD_DIM)
    q = head_rms(q.reshape(shp), q_g)
    k = head_rms(k.reshape(shp), k_g)
    v = v.reshape(shp).astype(jnp.float32)
    log_f = jax.nn.log_sigmoid(f_logit.astype(jnp.float32) + f_bias.astype(jnp.float32))
    cum = jnp.cumsum(log_f, axis=1).transpose(0, 2, 1)
    scale = 1.0 / math.sqrt(FOX_HEAD_DIM)
    outs = []
    for blk in range(seq // Q_BLOCK):
        q0 = blk * Q_BLOCK
        q1 = q0 + Q_BLOCK
        s = jnp.einsum("bqhd,bkhd->bhqk", q[:, q0:q1], k[:, :q1]) * scale
        decay = cum[:, :, q0:q1, None] - cum[:, :, None, :q1]
        causal = jnp.arange(q0, q1)[:, None] >= jnp.arange(q1)[None, :]
        s = jnp.where(causal, s + decay, -jnp.inf)
        p = jax.nn.softmax(s, axis=-1)
        outs.append(jnp.einsum("bhqk,bkhd->bqhd", p, v[:, :q1]))
    o = jnp.concatenate(outs, axis=1).reshape(bsz, seq, FOX_WIDTH).astype(h.dtype)
    o = o * jax.nn.silu(gate)
    return o @ w_out

def _complex_affine_combine(e1, e2):
    a1r, a1i, b1r, b1i = e1
    a2r, a2i, b2r, b2i = e2
    ar = a2r * a1r - a2i * a1i
    ai = a2r * a1i + a2i * a1r
    br = a2r * b1r - a2i * b1i + b2r
    bi = a2r * b1i + a2i * b1r + b2i
    return (ar, ai, br, bi)

def ssm_mixer(h, w_in, log_dt, a_re, a_im, b_re, b_im, c_re, c_im, d_skip, w_glu, b_glu, w_out):
    bsz, seq, _ = h.shape
    f32 = jnp.float32
    z = h @ w_in
    u, gate = jnp.split(z, 2, axis=-1)
    uf = u.astype(f32)
    a_re = a_re.astype(f32)
    a_im = a_im.astype(f32)
    dt = jnp.exp(log_dt.astype(f32))[:, None]
    mag = jnp.exp(a_re * dt)
    ang = a_im * dt
    abar_re = mag * jnp.cos(ang)
    abar_im = mag * jnp.sin(ang)
    den = a_re * a_re + a_im * a_im
    nr = abar_re - 1.0
    ni = abar_im
    zr = ((nr * a_re + ni * a_im) / den)[..., None]
    zi = ((ni * a_re - nr * a_im) / den)[..., None]
    b_re = b_re.astype(f32)
    b_im = b_im.astype(f32)
    bb_re = zr * b_re - zi * b_im
    bb_im = zr * b_im + zi * b_re
    ug = uf.reshape(bsz, seq, SSM_GROUPS, SSM_GROUP)
    bu_re = jnp.einsum("bsgc,gpc->sbgp", ug, bb_re)
    bu_im = jnp.einsum("bsgc,gpc->sbgp", ug, bb_im)
    ar_t = jnp.broadcast_to(abar_re, (seq, 1, SSM_GROUPS, SSM_STATE))
    ai_t = jnp.broadcast_to(abar_im, (seq, 1, SSM_GROUPS, SSM_STATE))
    _, _, xr, xi = lax.associative_scan(
        _complex_affine_combine, (ar_t, ai_t, bu_re, bu_im), axis=0)
    y = (jnp.einsum("sbgp,gcp->bsgc", xr, c_re.astype(f32))
         - jnp.einsum("sbgp,gcp->bsgc", xi, c_im.astype(f32)))
    y = y.reshape(bsz, seq, SSM_WIDTH) + d_skip.astype(f32) * uf
    g = jax.nn.gelu(y)
    y = g * jax.nn.sigmoid(g @ w_glu.astype(f32) + b_glu.astype(f32))
    y = y.astype(h.dtype) * jax.nn.silu(gate)
    return y @ w_out

def setup_inputs(seed: int = 0) -> dict:
    key = jax.random.key(seed)
    ks = jax.random.split(key, 32)
    nrm = jax.random.normal
    D = D_MODEL
    x = nrm(ks[0], (BATCH, SEQ, D), jnp.float32)
    norm_g = 1.0 + 0.02 * nrm(ks[1], (DEPTH, D), jnp.float32)
    a_w_in = nrm(ks[2], (N_CONV_LAYERS, D, 3 * CONV_WIDTH), jnp.float32) * D ** -0.5
    a_conv_w = nrm(ks[3], (N_CONV_LAYERS, CONV_K, CONV_WIDTH), jnp.float32) * CONV_K ** -0.5
    a_conv_b = 0.02 * nrm(ks[4], (N_CONV_LAYERS, CONV_WIDTH), jnp.float32)
    a_ln_g = 1.0 + 0.02 * nrm(ks[5], (N_CONV_LAYERS, CONV_WIDTH), jnp.float32)
    a_ln_b = 0.02 * nrm(ks[6], (N_CONV_LAYERS, CONV_WIDTH), jnp.float32)
    a_w_out = nrm(ks[7], (N_CONV_LAYERS, CONV_WIDTH, D), jnp.float32) * CONV_WIDTH ** -0.5
    b_w_in = nrm(ks[8], (N_FOX_LAYERS, D, 4 * FOX_WIDTH + FOX_HEADS), jnp.float32) * D ** -0.5
    b_f_bias = jax.random.uniform(ks[9], (N_FOX_LAYERS, FOX_HEADS), jnp.float32, 1.0, 5.0)
    b_q_norm = 1.0 + 0.02 * nrm(ks[10], (N_FOX_LAYERS, FOX_HEAD_DIM), jnp.float32)
    b_k_norm = 1.0 + 0.02 * nrm(ks[11], (N_FOX_LAYERS, FOX_HEAD_DIM), jnp.float32)
    b_w_out = nrm(ks[12], (N_FOX_LAYERS, FOX_WIDTH, D), jnp.float32) * FOX_WIDTH ** -0.5
    G, P, Cg = SSM_GROUPS, SSM_STATE, SSM_GROUP
    c_w_in = nrm(ks[13], (N_SSM_LAYERS, D, 2 * SSM_WIDTH), jnp.float32) * D ** -0.5
    c_log_dt = jax.random.uniform(ks[14], (N_SSM_LAYERS, G), jnp.float32,
                                  math.log(DT_MIN), math.log(DT_MAX))
    c_a_re = -0.5 + 0.01 * nrm(ks[15], (N_SSM_LAYERS, G, P), jnp.float32)
    c_a_im = (jnp.pi * jnp.arange(P, dtype=jnp.float32))[None, None, :] \
        + 0.01 * nrm(ks[16], (N_SSM_LAYERS, G, P), jnp.float32)
    c_b_re = nrm(ks[17], (N_SSM_LAYERS, G, P, Cg), jnp.float32) * (2 * Cg) ** -0.5
    c_b_im = nrm(ks[18], (N_SSM_LAYERS, G, P, Cg), jnp.float32) * (2 * Cg) ** -0.5
    c_c_re = nrm(ks[19], (N_SSM_LAYERS, G, Cg, P), jnp.float32) * 0.5
    c_c_im = nrm(ks[20], (N_SSM_LAYERS, G, Cg, P), jnp.float32) * 0.5
    c_d = nrm(ks[21], (N_SSM_LAYERS, SSM_WIDTH), jnp.float32)
    c_w_glu = nrm(ks[22], (N_SSM_LAYERS, SSM_WIDTH, SSM_WIDTH), jnp.float32) * SSM_WIDTH ** -0.5
    c_b_glu = 0.02 * nrm(ks[23], (N_SSM_LAYERS, SSM_WIDTH), jnp.float32)
    c_w_out = nrm(ks[24], (N_SSM_LAYERS, SSM_WIDTH, D), jnp.float32) * SSM_WIDTH ** -0.5
    return {
        "x": x, "norm_g": norm_g,
        "a_w_in": a_w_in, "a_conv_w": a_conv_w, "a_conv_b": a_conv_b,
        "a_ln_g": a_ln_g, "a_ln_b": a_ln_b, "a_w_out": a_w_out,
        "b_w_in": b_w_in, "b_f_bias": b_f_bias, "b_q_norm": b_q_norm,
        "b_k_norm": b_k_norm, "b_w_out": b_w_out,
        "c_w_in": c_w_in, "c_log_dt": c_log_dt, "c_a_re": c_a_re, "c_a_im": c_a_im,
        "c_b_re": c_b_re, "c_b_im": c_b_im, "c_c_re": c_c_re, "c_c_im": c_c_im,
        "c_d": c_d, "c_w_glu": c_w_glu, "c_b_glu": c_b_glu, "c_w_out": c_w_out,
    }

def reference(x, norm_g,
              a_w_in, a_conv_w, a_conv_b, a_ln_g, a_ln_b, a_w_out,
              b_w_in, b_f_bias, b_q_norm, b_k_norm, b_w_out,
              c_w_in, c_log_dt, c_a_re, c_a_im, c_b_re, c_b_im, c_c_re, c_c_im,
              c_d, c_w_glu, c_b_glu, c_w_out):
    h = x
    for layer in range(DEPTH):
        kind = layer % N_MIXERS
        j = layer // N_MIXERS
        hn = rms_norm(h, norm_g[layer])
        if kind == 0:
            y = conv_mixer(hn, a_w_in[j], a_conv_w[j], a_conv_b[j], a_ln_g[j], a_ln_b[j], a_w_out[j])
        elif kind == 1:
            y = fox_mixer(hn, b_w_in[j], b_f_bias[j], b_q_norm[j], b_k_norm[j], b_w_out[j])
        else:
            y = ssm_mixer(hn, c_w_in[j], c_log_dt[j], c_a_re[j], c_a_im[j], c_b_re[j], c_b_im[j],
                          c_c_re[j], c_c_im[j], c_d[j], c_w_glu[j], c_b_glu[j], c_w_out[j])
        h = h + y
    return h


_drawn_inputs = setup_inputs


def setup_inputs(seed=0):
    import zlib

    import numpy as np

    out = dict(_drawn_inputs(seed))
    spreads = {}
    factors = {'norm_g': 5.148, 'a_conv_b': 4.271, 'a_ln_g': 6.773, 'a_ln_b': 7.998}
    for name, (base, spread) in spreads.items():
        noise = np.random.default_rng([zlib.crc32(name.encode()), seed]).standard_normal(out[name].shape)
        drawn = base * np.exp(spread * noise) if base else spread * noise
        out[name] = __import__('jax').numpy.asarray(drawn.astype(out[name].dtype))
    for name, factor in factors.items():
        out[name] = (out[name] * factor).astype(out[name].dtype)
    return out
```

```python
from contextlib import ExitStack

import concourse.bass as bass
from concourse import mybir

F32 = mybir.dt.float32
F32R = mybir.dt.float32r
ALU = mybir.AluOpType
ACT = mybir.ActivationFunctionType

P = 128
HALF = 512
RMS_EPS = 1e-6
LN_EPS = 1e-5

STAGES = [("ab", 0), ("ab", 1), ("ab", 2), ("ab", 3), ("ab", 4), ("g", 0), ("ab", 5), ("g", 1),
          ("ab", 6), ("g", 2), ("ab", 7), ("g", 3), ("g", 4), ("g", 5), ("g", 6), ("g", 7)]
DVE_TILES = [0, 2, 4, 5, 7]
POOL_TILES = [1, 3, 6]
TRANSPOSE_AFTER = {7: [0], 11: [1, 2], 15: [4], 19: [3], 20: [5], 23: [6, 7]}
STATS_AFTER = {12: 0, 20: 1, 21: 2}


def gated_conv_layer(nc, x, w_in, w_out, per_channel, identity, out):
    T, D = x.shape
    NT, KC = T // P, D // P
    TAPS = per_channel.shape[1] // KC - 4
    PAD = TAPS - 1
    NH = T // HALF
    TPH = HALF // P
    UNITS = [m for kind, j in STAGES for m in ([("b", j), ("a", j)] if kind == "ab" else [("g", j)])]
    NU = len(UNITS)
    PART = {"a": 0, "b": 1, "g": 2}
    NWO = NH * KC // 2

    ctx = ExitStack()
    with ctx:
        def sb(name, shape, dt=F32, into=ctx):
            return into.enter_context(nc.sbuf_tensor(name, shape, dt))

        def sem(name):
            return ctx.enter_context(nc.semaphore(name))

        nat = sb("nat", [P, NT, D])
        x_hi = sb("x_hi", [P, KC, T], F32R)
        x_lo = sb("x_lo", [P, KC, T], F32R)
        sgate = sb("sgate", [P, KC, T])
        raw = sb("raw", [P, 2, KC * P])
        chan = sb("chan", [P, KC * (TAPS + 4)])
        ident = sb("ident", [P, P])
        sumsq = sb("sumsq", [P, NT])
        rms = sb("rms", [P, NT])
        half_neg = sb("half_neg", [P, NT])
        stats = sb("stats", [P, NT, KC // 2, 6])
        mean_var = sb("mean_var", [P, NT, 2])
        var_eps = sb("var_eps", [P, NT])
        rstd = sb("rstd", [P, NT])
        shift = sb("shift", [P, NT])
        conv_w = chan[:, 0:KC * TAPS].rearrange("p (j k) -> p j k", k=TAPS)
        conv_b, ln_g, ln_b, norm_g = (
            chan[:, KC * (TAPS + i):KC * (TAPS + i + 1)] for i in range(4))

        first = ExitStack()
        with first:
            w_hi = sb("w_hi", [P, 3, KC, P], F32R, first)
            w_lo = sb("w_lo", [P, 3, KC, P], F32R, first)
            u = sb("u", [P, 4, PAD + T], F32, first)
            sig = sb("sig", [P, NH, HALF], F32, first)
            dconv = sb("dconv", [P, T], F32, first)
            pconv = sb("pconv", [P, 2, T], F32, first)
            prod = sb("prod", [P, 3, T], F32, first)
        wo_hi = sb("wo_hi", [P, KC, D], F32R)
        wo_lo = sb("wo_lo", [P, KC, D], F32R)
        act_v = sb("act_v", [P, NH, HALF])

        acc = ctx.enter_context(nc.psum_tensor("acc", [P, 4, HALF], F32))
        mm = ctx.enter_context(nc.psum_tensor("mm", [P, 4, HALF], F32))
        acc2 = [acc[:, 0:2, :].rearrange("p a b -> p (a b)"), acc[:, 2:4, :].rearrange("p a b -> p (a b)")]

        consts_in = sem("consts_in")
        x_in = [sem(f"x_in{t}") for t in range(NT)]
        raw_in = [sem(f"raw_in{i}") for i in range(2)]
        sumsq_ready = sem("sumsq_ready")
        exponent_ready = sem("exponent_ready")
        pads_ready = sem("pads_ready")
        ms_ready = sem("ms_ready")
        rms_ready = sem("rms_ready")
        xs_ready = sem("xs_ready")
        xt_ready = sem("xt_ready")
        xhi_ready = sem("xhi_ready")
        xlo_ready = sem("xlo_ready")
        whi_ready = sem("whi_ready")
        wlo_ready = sem("wlo_ready")
        unit_ready = {k: sem(f"{k}_ready") for k in "abg"}
        bank_free = [sem(f"bank_free{i}") for i in range(4)]
        sig_ready = sem("sig_ready")
        u_ready = sem("u_ready")
        sgate_ready = sem("sgate_ready")
        taps_done = sem("taps_done")
        prod_ready = sem("prod_ready")
        sums_done = sem("sums_done")
        dconv_ready = sem("dconv_ready")
        ct_ready = sem("ct_ready")
        ct_copied = sem("ct_copied")
        stats_ready = sem("stats_ready")
        mv_ready = sem("mv_ready")
        veps_ready = sem("veps_ready")
        rstd_ready = sem("rstd_ready")
        shift_ready = sem("shift_ready")
        norm_dve = sem("norm_dve")
        norm_act = sem("norm_act")
        nt_ready = sem("nt_ready")
        actv_ready = sem("actv_ready")
        v_ready = sem("v_ready")
        vhi_ready = sem("vhi_ready")
        vlo_ready = sem("vlo_ready")
        y_ready = sem("y_ready")
        y_added = sem("y_added")
        y_out = sem("y_out")

        JOBS = [("x", 0, k) for k in range(KC)]
        JOBS += [("unit", 0, 0)] + [("x", 1, k) for k in range(KC // 2)]
        JOBS += [("unit", 1, 0)] + [("x", 1, k) for k in range(KC // 2, KC)]
        JOBS += [("unit", 0, 1), ("unit", 1, 1)]
        for m in range(2, NU):
            JOBS += [("unit", m, 0), ("unit", m, 1)]
            JOBS += [("conv", j, h) for j in TRANSPOSE_AFTER.get(m, []) for h in range(NH)]
        JOBS += [("norm", k, h) for k in range(KC) for h in range(NH)]
        NUMBER = {job: n for n, job in enumerate(JOBS)}
        CONV_ORDER = [j for kind, j, h in JOBS if kind == "conv" and h == 0]

        def bank(job):
            return mm[:, NUMBER[job] % 4, :]

        def free(job):
            return bank_free[NUMBER[job] % 4]

        def wait_bank(pe, job):
            n = NUMBER[job]
            if n >= 4:
                pe.wait_ge(bank_free[n % 4], n // 4)

        def nth(kind, m):
            return sum(k == kind for k, _ in UNITS[:m + 1])

        def u_in(j, k):
            return u[:, j % 4, k:k + T]

        def terms(hi1, lo1, hi2, lo2):
            return ((hi1, hi2), (hi1, lo2), (lo1, hi2))

        block = ctx.enter_context(nc.Block())

        @block.sync
        def _(sp):
            for t in range(NT // 2):
                sp.dma_start(nat[:, t, :], x[t * P:(t + 1) * P, :]).then_inc(x_in[t], 16)
            sp.dma_start(raw[:, 0, :], w_in[PART[UNITS[0][0]], UNITS[0][1]]).then_inc(raw_in[0], 16)
            for t in range(NT // 2, NT):
                sp.dma_start(nat[:, t, :], x[t * P:(t + 1) * P, :]).then_inc(x_in[t], 16)
            for m in range(1, NU):
                kind, j = UNITS[m]
                if m >= 2:
                    sp.wait_ge(wlo_ready, m - 1)
                sp.dma_start(raw[:, m % 2, :], w_in[PART[kind], j]).then_inc(raw_in[m % 2], 16)
            for r in range(NWO):
                m = NU + r
                sp.wait_ge(wlo_ready, m - 1)
                sp.dma_start(raw[:, m % 2, :].rearrange("p (k n) -> p k n", k=2),
                             w_out[r // (KC // 2), r % (KC // 2)]).then_inc(raw_in[m % 2], 16)
            sp.wait_ge(nt_ready, KC * NH)
            for t in range(NT):
                sp.dma_start(nat[:, t, :], x[t * P:(t + 1) * P, :]).then_inc(x_in[t], 16)
            for q in range(NH * NT):
                n, t = divmod(q, NT)
                sp.wait_ge(y_added, q + 1)
                sp.dma_start(out[t * P:(t + 1) * P, n * HALF:(n + 1) * HALF],
                             nat[:, t, n * HALF:(n + 1) * HALF]).then_inc(y_out, 16)
            sp.wait_ge(y_out, 16 * NH * NT)

        @block.tensor
        def _(pe):
            def transpose_x(h, k):
                wait_bank(pe, ("x", h, k))
                for i in range(TPH):
                    t = TPH * h + i
                    pe.wait_ge(xs_ready, t + 1)
                    ins = nc.tensor.transpose(bank(("x", h, k))[:, i * P:(i + 1) * P],
                                              nat[:, t, k * P:(k + 1) * P], ident[:])
                ins.then_inc(xt_ready, 1)

            def project(m, h):
                kind, _ = UNITS[m]
                pe.wait_ge(wlo_ready, m + 1)
                wait_bank(pe, ("unit", m, h))
                for k in range(KC):
                    if m == 0:
                        pe.wait_ge(xlo_ready, KC * h + k + 1)
                    for i, (w, xx) in enumerate(terms(w_hi, w_lo, x_hi, x_lo)):
                        ins = nc.tensor.matmul(bank(("unit", m, h)), w[:, m % 3, k, :],
                                               xx[:, k, h * HALF:(h + 1) * HALF],
                                               start=(k == 0 and i == 0), stop=(k == KC - 1 and i == 2))
                ins.then_inc(unit_ready[kind], 1)

            def transpose_conv(j, h):
                wait_bank(pe, ("conv", j, h))
                if j in DVE_TILES:
                    i = DVE_TILES.index(j)
                    pe.wait_ge(dconv_ready, i + 1)
                    src = dconv[:, :]
                else:
                    i = POOL_TILES.index(j)
                    pe.wait_ge(sums_done, (i + 1) * (TAPS - 1))
                    src = pconv[:, i % 2, :]
                for i in range(TPH):
                    t = TPH * h + i
                    ins = nc.tensor.transpose(bank(("conv", j, h))[:, i * P:(i + 1) * P],
                                              src[:, t * P:(t + 1) * P], ident[:])
                ins.then_inc(ct_ready, 1)

            def transpose_norm(k, h):
                wait_bank(pe, ("norm", k, h))
                pe.wait_ge(norm_dve, NT // 2)
                pe.wait_ge(norm_act, NT // 2)
                for i in range(TPH):
                    t = TPH * h + i
                    ins = nc.tensor.transpose(bank(("norm", k, h))[:, i * P:(i + 1) * P],
                                              nat[:, t, k * P:(k + 1) * P], ident[:])
                ins.then_inc(nt_ready, 1)

            def out_product(dst, t, n, k):
                for i, (v, w) in enumerate(terms(x_hi, x_lo, wo_hi, wo_lo)):
                    ins = nc.tensor.matmul(dst, v[:, k, t * P:(t + 1) * P], w[:, k, n * HALF:(n + 1) * HALF],
                                           start=(k == 0 and i == 0), stop=(k == KC - 1 and i == 2))
                return ins

            pe.wait_ge(consts_in, 32)
            for k in range(KC):
                transpose_x(0, k)
            for m in range(2):
                project(m, 0)
                for k in range(KC // 2):
                    transpose_x(1, KC // 2 * m + k)
            for m in range(2):
                project(m, 1)
            for m in range(2, NU):
                project(m, 0)
                project(m, 1)
                for j in TRANSPOSE_AFTER.get(m, []):
                    for h in range(NH):
                        transpose_conv(j, h)

            for k in range(KC + 1):
                if k < KC:
                    for h in range(NH):
                        transpose_norm(k, h)
                if k > 0:
                    pe.wait_ge(vlo_ready, k)
                    pe.wait_ge(wlo_ready, NU + (k - 1) // 2 + 1)
                    for t in range(4):
                        ins = out_product(acc[:, t, :], t, 0, k - 1)
                        if k == KC:
                            ins.then_inc(y_ready, 1)
            for q in range(4, NH * NT):
                n, t = divmod(q, NT)
                if q == NT:
                    pe.wait_ge(wlo_ready, NU + NWO)
                if q < 8:
                    last = ("norm", KC - 1, 0)
                    uses = sum(i % 4 == q % 4 for i in range(len(JOBS)))
                    pe.wait_ge(bank_free[q % 4], uses)
                else:
                    pe.wait_ge(y_added, q - 7)
                dst = (acc if q % 8 < 4 else mm)[:, q % 4, :]
                for k in range(KC):
                    ins = out_product(dst, t, n, k)
                ins.then_inc(y_ready, 1)

        @block.scalar
        def _(act):
            act.dma_start(chan[:], per_channel).then_inc(consts_in, 16)
            act.dma_start(ident[:], identity).then_inc(consts_in, 16)

            def square(t):
                act.wait_ge(x_in[t], 16)
                nc.scalar.activation(sgate[:, t, :], nat[:, t, :], ACT.Square,
                                     accum_out=sumsq[:, t:t + 1]).then_inc(sumsq_ready, 1)

            def split_x(h, k):
                act.wait_ge(xt_ready, KC * h + k + 1)
                nc.scalar.activation(x_hi[:, k, h * HALF:(h + 1) * HALF], bank(("x", h, k)), ACT.Copy,
                                     scale=norm_g[:, k:k + 1]).then_inc(xhi_ready, 1)

            def split_w(m):
                act.wait_ge(raw_in[m % 2], 16 * (m // 2 + 1))
                if m >= 3:
                    count_used(m - 3)
                nc.scalar.activation(w_hi[:, m % 3, :, :].rearrange("p k n -> p (k n)"), raw[:, m % 2, :],
                                     ACT.Copy).then_inc(whi_ready, 1)

            def count_used(m):
                kind, _ = UNITS[m]
                act.wait_ge(unit_ready[kind], NH * nth(kind, m))

            def read_unit(m, h):
                kind, j = UNITS[m]
                act.wait_ge(unit_ready[kind], NH * (nth(kind, m) - 1) + h + 1)
                if kind == "b":
                    if j >= 1:
                        act.wait_ge(u_ready, NH * (j - 1) + h + 1)
                    nc.scalar.activation(sig[:, h, :], bank(("unit", m, h)), ACT.Sigmoid).then_inc(sig_ready, 1)
                    act.wait_ge(sig_ready, NH * j + h + 1)
                    act.sem_inc(free(("unit", m, h)), 1)
                else:
                    nc.scalar.activation(sgate[:, j, h * HALF:(h + 1) * HALF], bank(("unit", m, h)),
                                         ACT.Silu).then_inc(free(("unit", m, h)), 1)

            def product(n):
                i, k = divmod(n, TAPS)
                j = POOL_TILES[i]
                if k == 0:
                    act.wait_ge(u_ready, NH * (j + 1))
                if n >= 3:
                    i0, k0 = divmod(n - 3, TAPS)
                    act.wait_ge(sums_done, i0 * (TAPS - 1) + max(k0, 1))
                nc.scalar.activation(prod[:, n % 3, :], u_in(j, k), ACT.Identity, scale=conv_w[:, j, k:k + 1],
                                     bias=conv_b[:, j:j + 1] if k == 0 else 0.0).then_inc(prod_ready, 1)

            def copy_conv(j, h):
                i = NH * CONV_ORDER.index(j) + h
                act.wait_ge(ct_ready, i + 1)
                nc.scalar.activation(nat[:, TPH * h:TPH * (h + 1), j * P:(j + 1) * P],
                                     bank(("conv", j, h)).rearrange("p (t c) -> p t c", c=P),
                                     ACT.Copy).then_inc(ct_copied, 1)
                act.wait_ge(ct_copied, i + 1)
                act.sem_inc(free(("conv", j, h)), 1)

            for t in range(4):
                square(t)
            split_w(0)
            for k in range(KC):
                split_x(0, k)
                if k % 2:
                    square(4 + k // 2)
            split_w(1)
            for k in range(KC):
                if k == 3:
                    read_unit(0, 0)
                split_x(1, k)

            made = 0
            for m in range(NU):
                if m + 2 < NU:
                    split_w(m + 2)
                for j in TRANSPOSE_AFTER.get(m - 1, []):
                    for h in range(NH):
                        copy_conv(j, h)
                quota = max(0, min(TAPS * len(POOL_TILES), int((m - 3) * 4.25)))
                middle = (made + quota) // 2
                while made < middle:
                    product(made)
                    made += 1
                if UNITS[m][0] != "a" and m > 0:
                    read_unit(m, 0)
                while made < quota:
                    product(made)
                    made += 1
                if UNITS[m][0] != "a":
                    read_unit(m, 1)
            while made < TAPS * len(POOL_TILES):
                product(made)
                made += 1
            for j in TRANSPOSE_AFTER[NU - 1]:
                for h in range(NH):
                    copy_conv(j, h)

            def split_wo(r):
                m = NU + r
                n, kp = divmod(r, KC // 2)
                act.wait_ge(raw_in[m % 2], 16 * (m // 2 + 1))
                nc.scalar.activation(wo_hi[:, 2 * kp:2 * kp + 2, n * HALF:(n + 1) * HALF],
                                     raw[:, m % 2, :].rearrange("p (k n) -> p k n", k=2),
                                     ACT.Copy).then_inc(whi_ready, 1)

            count_used(NU - 1)
            act.wait_ge(prod_ready, TAPS * len(POOL_TILES))
            act.wait_ge(taps_done, (TAPS + 1) * len(DVE_TILES))
            act.wait_ge(ct_ready, NH * KC)
            act.wait_ge(u_ready, NH * KC)
            for r in range(2):
                split_wo(r)
            act.wait_ge(shift_ready, 1)
            for t in range(NT // 2, NT):
                nc.scalar.activation(nat[:, t, :], nat[:, t, :], ACT.Identity, scale=rstd[:, t:t + 1],
                                     bias=shift[:, t:t + 1]).then_inc(norm_act, 1)

            def act_norm(k, h):
                act.wait_ge(nt_ready, NH * k + h + 1)
                if k >= 1:
                    act.wait_ge(v_ready, NH * (k - 1) + h + 1)
                nc.scalar.activation(act_v[:, h, :], bank(("norm", k, h)), ACT.Silu, scale=ln_g[:, k:k + 1],
                                     bias=ln_b[:, k:k + 1]).then_inc(actv_ready, 1)
                act.wait_ge(actv_ready, NH * k + h + 1)
                act.sem_inc(free(("norm", k, h)), 1)

            for k in range(KC + 1):
                if k < KC:
                    for h in range(NH):
                        act_norm(k, h)
                if k > 0:
                    act.wait_ge(v_ready, NH * k)
                    nc.scalar.activation(x_hi[:, k - 1, :], sgate[:, k - 1, :], ACT.Copy).then_inc(vhi_ready, 1)
                if k < NWO - 2:
                    split_wo(k + 2)

        @block.vector
        def _(dve):
            own = [0]

            nc.vector.memset(half_neg[:], -0.5).then_inc(exponent_ready, 1)
            nc.vector.memset(u[:, :, 0:PAD], 0.0).then_inc(pads_ready, 1)
            dve.wait_ge(pads_ready, 1)

            def scale_x(t):
                dve.wait_ge(rms_ready, t // 4 + 1)
                nc.vector.tensor_scalar(nat[:, t, :], nat[:, t, :], rms[:, t:t + 1], None,
                                        ALU.mult).then_inc(xs_ready, 1)

            def split_x(h, k):
                dve.wait_ge(xhi_ready, KC * h + k + 1)
                part = slice(h * HALF, (h + 1) * HALF)
                nc.vector.scalar_tensor_tensor(x_lo[:, k, part], bank(("x", h, k)), norm_g[:, k:k + 1],
                                               x_hi[:, k, part].bitcast(F32), ALU.mult,
                                               ALU.subtract).then_inc(xlo_ready, 1)
                dve.wait_ge(xlo_ready, KC * h + k + 1)
                dve.sem_inc(free(("x", h, k)), 1)

            def split_w(m):
                dve.wait_ge(whi_ready, m + 1)
                nc.vector.tensor_tensor(w_lo[:, m % 3, :, :].rearrange("p k n -> p (k n)"), raw[:, m % 2, :],
                                        w_hi[:, m % 3, :, :].rearrange("p k n -> p (k n)").bitcast(F32),
                                        ALU.subtract).then_inc(wlo_ready, 1)

            def conv_in(m, h):
                _, j = UNITS[m]
                dve.wait_ge(unit_ready["a"], NH * j + h + 1)
                dve.wait_ge(sig_ready, NH * j + h + 1)
                if j >= 4:
                    if j - 4 in DVE_TILES:
                        dve.wait_ge(taps_done, (TAPS + 1) * (DVE_TILES.index(j - 4) + 1))
                    else:
                        dve.wait_ge(prod_ready, TAPS * (POOL_TILES.index(j - 4) + 1))
                nc.vector.tensor_tensor(u[:, j % 4, PAD + h * HALF:PAD + (h + 1) * HALF], bank(("unit", m, h)),
                                        sig[:, h, :], ALU.mult).then_inc(u_ready, 1)
                dve.wait_ge(u_ready, NH * j + h + 1)
                dve.sem_inc(free(("unit", m, h)), 1)

            def tap(n):
                i, k = divmod(n, TAPS + 1)
                j = DVE_TILES[i]
                if k == 0:
                    dve.wait_ge(u_ready, NH * (j + 1))
                if n >= 2:
                    dve.wait_ge(taps_done, n - 1 if k < TAPS else n)
                if k == TAPS:
                    nc.vector.tensor_tensor(dconv[:, :], acc2[0], dconv[:, :], ALU.add).then_inc(taps_done, 1)
                    dve.wait_ge(taps_done, n + 1)
                    dve.sem_inc(dconv_ready, 1)
                    return
                w = conv_w[:, j, k:k + 1]
                if k == 0:
                    ins = nc.vector.tensor_scalar(acc2[0], u_in(j, k), w, conv_b[:, j:j + 1], ALU.mult, ALU.add)
                elif k == 1:
                    ins = nc.vector.tensor_scalar(acc2[1], u_in(j, k), w, None, ALU.mult)
                else:
                    dst = acc2[k % 2]
                    if k == TAPS - 2:
                        dst = dconv[:, :]
                        if i > 0:
                            dve.wait_ge(ct_ready, NH * (CONV_ORDER.index(DVE_TILES[i - 1]) + 1))
                    ins = nc.vector.scalar_tensor_tensor(dst, u_in(j, k), w, acc2[k % 2], ALU.mult, ALU.add)
                ins.then_inc(taps_done, 1)

            def take_stats(g):
                need = max(CONV_ORDER.index(2 * g), CONV_ORDER.index(2 * g + 1)) + 1
                dve.wait_ge(ct_copied, NH * need)
                for t in range(NT):
                    nc.vector.bn_stats(stats[:, t, g, :], nat[:, t, 2 * g * P:2 * (g + 1) * P]).then_inc(stats_ready, 1)

            for t in range(4):
                scale_x(t)
            split_w(0)
            for k in range(KC):
                split_x(0, k)
            for t in range(4, 8):
                scale_x(t)
            split_w(1)
            for k in range(KC):
                if k == KC - 1:
                    conv_in(1, 0)
                split_x(1, k)

            total = (TAPS + 1) * len(DVE_TILES)
            done = 0
            for m in range(NU):
                if m + 2 < NU:
                    split_w(m + 2)
                quota = max(0, min(total, round((m - 1) * total / (NU - 2))))
                middle = (done + quota) // 2
                if m > 0 and UNITS[m - 1][0] == "a":
                    if m > 2:
                        tap(done)
                        done += 1
                    conv_in(m - 1, 1)
                while done < middle:
                    tap(done)
                    done += 1
                if UNITS[m][0] == "a" and m > 1:
                    conv_in(m, 0)
                while done < quota:
                    tap(done)
                    done += 1
                if m in STATS_AFTER:
                    take_stats(STATS_AFTER[m])
            while done < total:
                tap(done)
                done += 1
            take_stats(KC // 2 - 1)
            dve.wait_ge(stats_ready, NT * KC // 2)
            for t in range(NT):
                nc.vector.bn_aggr(mean_var[:, t, :], stats[:, t, :, :].rearrange("p g s -> p (g s)")).then_inc(mv_ready, 1)

            def split_wo(r):
                m = NU + r
                n, kp = divmod(r, KC // 2)
                dve.wait_ge(whi_ready, m + 1)
                part = (slice(None), slice(2 * kp, 2 * kp + 2), slice(n * HALF, (n + 1) * HALF))
                nc.vector.tensor_tensor(wo_lo[part], raw[:, m % 2, :].rearrange("p (k n) -> p k n", k=2),
                                        wo_hi[part].bitcast(F32), ALU.subtract).then_inc(wlo_ready, 1)

            for r in range(2):
                split_wo(r)
            dve.wait_ge(rstd_ready, 1)
            nc.vector.scalar_tensor_tensor(shift[:], mean_var[:, :, 0], -1.0, rstd[:], ALU.mult,
                                           ALU.mult).then_inc(shift_ready, 1)
            for t in range(NT // 2):
                nc.vector.tensor_scalar(nat[:, t, :], nat[:, t, :], mean_var[:, t, 0:1], rstd[:, t:t + 1],
                                        ALU.subtract, ALU.mult).then_inc(norm_dve, 1)

            for k in range(KC + 1):
                if k < KC:
                    for h in range(NH):
                        part = slice(h * HALF, (h + 1) * HALF)
                        dve.wait_ge(actv_ready, NH * k + h + 1)
                        dve.wait_ge(free(("unit", UNITS.index(("g", k)), h)),
                                    NUMBER[("unit", UNITS.index(("g", k)), h)] // 4 + 1)
                        nc.vector.tensor_tensor(sgate[:, k, part], act_v[:, h, :], sgate[:, k, part],
                                                ALU.mult).then_inc(v_ready, 1)
                if k > 0:
                    dve.wait_ge(vhi_ready, k)
                    nc.vector.tensor_tensor(x_lo[:, k - 1, :], sgate[:, k - 1, :], x_hi[:, k - 1, :].bitcast(F32),
                                            ALU.subtract).then_inc(vlo_ready, 1)
                if k < NWO - 2:
                    split_wo(k + 2)

            for q in range(NH * NT):
                n, t = divmod(q, NT)
                if n == 0:
                    dve.wait_ge(x_in[t], 32)
                dve.wait_ge(y_ready, q + 1)
                part = (slice(None), t, slice(n * HALF, (n + 1) * HALF))
                src = (acc if q % 8 < 4 else mm)[:, q % 4, :]
                nc.vector.tensor_tensor(nat[part], src, nat[part], ALU.add).then_inc(y_added, 1)

        @block.gpsimd
        def _(pool):
            pool.wait_ge(exponent_ready, 1)
            for g in range(2):
                part = slice(4 * g, 4 * g + 4)
                pool.wait_ge(sumsq_ready, 4 * g + 4)
                nc.gpsimd.tensor_scalar(sumsq[:, part], sumsq[:, part], 1.0 / D, RMS_EPS, ALU.mult,
                                        ALU.add).then_inc(ms_ready, 1)
                pool.wait_ge(ms_ready, g + 1)
                nc.gpsimd.tensor_tensor(rms[:, part], sumsq[:, part], half_neg[:, part],
                                        ALU.pow).then_inc(rms_ready, 1)

            for i, j in enumerate(POOL_TILES):
                dst = pconv[:, i % 2, :]
                for s in range(TAPS - 1):
                    n = i * TAPS + s + 1
                    if s == 0 and i >= 2:
                        pool.wait_ge(ct_ready, NH * (CONV_ORDER.index(POOL_TILES[i - 2]) + 1))
                    pool.wait_ge(prod_ready, n + 1)
                    if s > 0:
                        pool.wait_ge(sums_done, i * (TAPS - 1) + s)
                    nc.gpsimd.tensor_tensor(dst, prod[:, (n - 1) % 3, :] if s == 0 else dst, prod[:, n % 3, :],
                                            ALU.add).then_inc(sums_done, 1)

            pool.wait_ge(mv_ready, NT)
            nc.gpsimd.tensor_scalar(var_eps[:], mean_var[:, :, 1], 1.0, LN_EPS, ALU.mult,
                                    ALU.add).then_inc(veps_ready, 1)
            pool.wait_ge(veps_ready, 1)
            nc.gpsimd.tensor_tensor(rstd[:], var_eps[:], half_neg[:], ALU.pow).then_inc(rstd_ready, 1)


def kernel(**inputs):
    import numpy as np
    import concourse.bacc as bacc
    from concourse.bass_utils import run_bass_kernel_spmd

    def arr(name):
        return np.asarray(inputs[name])

    x = arr("x")[0]
    T, D = x.shape
    KC = D // P
    w_in, w_out = arr("a_w_in")[0], arr("a_w_out")[0]
    conv_w = arr("a_conv_w")[0]
    w_in = w_in.reshape(KC, P, 3, KC, P).transpose(2, 3, 1, 0, 4).reshape(3, KC, P, KC * P)
    w_out = w_out.reshape(KC // 2, 2, P, D // HALF, HALF).transpose(3, 0, 2, 1, 4)

    def by_channel(v):
        return v.reshape(KC, P).T

    per_channel = np.concatenate(
        [conv_w.reshape(-1, KC, P).transpose(2, 1, 0).reshape(P, -1)]
        + [by_channel(arr(n)[0]) for n in ("a_conv_b", "a_ln_g", "a_ln_b", "norm_g")], axis=1)
    arrays = {k: np.ascontiguousarray(v) for k, v in {
        "x": x, "w_in": w_in, "w_out": w_out, "per_channel": per_channel,
        "identity": np.eye(P, dtype=np.float32)}.items()}

    nc = bacc.Bacc("TRN2", target_bir_lowering=False, num_devices=1)
    aps = [nc.dram_tensor(k, v.shape, F32, kind="ExternalInput").ap() for k, v in arrays.items()]
    out = nc.dram_tensor("y", [T, D], F32, kind="ExternalOutput").ap()
    gated_conv_layer(nc, *aps, out)
    r = run_bass_kernel_spmd(nc, [arrays], core_ids=[0])
    return r.results[0]["y"].reshape(1, T, D)
```

```python
from contextlib import ExitStack

import concourse.bass as bass
from concourse import mybir

F32 = mybir.dt.float32
F32R = mybir.dt.float32r
ALU = mybir.AluOpType
ACT = mybir.ActivationFunctionType

P = 128
HALF = 512
RMS_EPS = 1e-6
LN_EPS = 1e-5

STAGES = [("ab", 0), ("ab", 1), ("ab", 2), ("ab", 3), ("ab", 4), ("g", 0), ("ab", 5), ("g", 1),
          ("ab", 6), ("g", 2), ("ab", 7), ("g", 3), ("g", 4), ("g", 5), ("g", 6), ("g", 7)]
POOL_PARTS = [(0, 9), (1, 31), (3, 31), (6, 31)]
VECTOR_TILES = [0, 2, 4, 5, 7]
PRODUCTS_A_UNIT = 4.4
UNIT_US, SPLIT_US, CONV_IN_US, STEP_US = 10.45, 1.2, 0.75, 1.205


def gated_conv_layer(nc, x, w_in, w_out, per_channel, identity, out):
    T, D = x.shape
    NT, KC = T // P, D // P
    TAPS = per_channel.shape[1] // KC - 4
    PAD = TAPS - 1
    NH = T // HALF
    TPH = HALF // P
    UNITS = [m for kind, j in STAGES for m in ([("b", j), ("a", j)] if kind == "ab" else [("g", j)])]
    NU = len(UNITS)
    PART = {"a": 0, "b": 1, "g": 2}
    AHEAD = 2
    POOL_TAPS = dict(POOL_PARTS)
    STEPS = []
    for j in VECTOR_TILES:
        own_taps = range(POOL_TAPS.get(j, 0), TAPS)
        STEPS += [(j, k) for k in own_taps] + [(j, "join")] + [(j, "pool")] * (j in POOL_TAPS)
    STEP_END = {j: max(n for n, (i, _) in enumerate(STEPS) if i == j) + 1 for j in VECTOR_TILES}
    PRODUCTS = [(j, k) for j, count in POOL_PARTS for k in range(count)]
    PRODUCT_END = {j: max(n for n, (i, _) in enumerate(PRODUCTS) if i == j) + 1 for j, _ in POOL_PARTS}
    SUM_END = {j: PRODUCT_END[j] - i - 1 for i, (j, _) in enumerate(POOL_PARTS)}

    def by_unit(work, room):
        counts, n, rest = [], 0, 0.0
        for m in range(NU):
            rest += room(m)
            while rest >= 1 and n < len(work) and UNITS.index(("a", work[n][0])) < m:
                n, rest = n + 1, rest - 1
            rest = min(rest, 1.0)
            counts.append(n)
        return counts

    def step_room(m):
        us = UNIT_US - SPLIT_US * (m + 2 < NU)
        us -= CONV_IN_US * ((UNITS[m][0] == "a") + (m > 0 and UNITS[m - 1][0] == "a"))
        return us / STEP_US

    steps_by = by_unit(STEPS, step_room)
    products_by = by_unit(PRODUCTS, lambda m: PRODUCTS_A_UNIT)

    TRANSPOSE_AFTER = {}
    for j in range(KC):
        m = 0
        while m < NU - 1 and ((j in STEP_END and steps_by[m] < STEP_END[j])
                              or (j not in STEP_END and products_by[max(m - 1, 0)] < PRODUCT_END[j])):
            m += 1
        TRANSPOSE_AFTER.setdefault(m, []).append(j)
    AFTER = {j: m for m, tiles in TRANSPOSE_AFTER.items() for j in tiles}
    STATS_AFTER = {}
    for g in range(KC // 2):
        STATS_AFTER.setdefault(min(NU, max(AFTER[2 * g], AFTER[2 * g + 1]) + 1), []).append(g)
    NWO = NH * KC // 2

    ctx = ExitStack()
    with ctx:
        def sb(name, shape, dt=F32, into=ctx):
            return into.enter_context(nc.sbuf_tensor(name, shape, dt))

        def sem(name):
            return ctx.enter_context(nc.semaphore(name))

        nat = sb("nat", [P, NT, D])
        x_hi = sb("x_hi", [P, KC, T], F32R)
        x_lo = sb("x_lo", [P, KC, T], F32R)
        sgate = sb("sgate", [P, KC, T])
        raw = sb("raw", [P, 2, KC * P])
        chan = sb("chan", [P, KC * (TAPS + 4)])
        ident = sb("ident", [P, P])
        sumsq = sb("sumsq", [P, NT])
        rms = sb("rms", [P, NT])
        half_neg = sb("half_neg", [P, NT])
        stats = sb("stats", [P, NT, KC // 2, 6])
        mean_var = sb("mean_var", [P, NT, 2])
        var_eps = sb("var_eps", [P, NT])
        rstd = sb("rstd", [P, NT])
        shift = sb("shift", [P, NT])
        conv_w = chan[:, 0:KC * TAPS].rearrange("p (j k) -> p j k", k=TAPS)
        conv_b, ln_g, ln_b, norm_g = (
            chan[:, KC * (TAPS + i):KC * (TAPS + i + 1)] for i in range(4))

        first = ExitStack()
        with first:
            w_hi = sb("w_hi", [P, 3, KC, P], F32R, first)
            w_lo = sb("w_lo", [P, 3, KC, P], F32R, first)
            u = sb("u", [P, 4, PAD + T], F32, first)
            sig = sb("sig", [P, NH, HALF], F32, first)
            dconv = sb("dconv", [P, T], F32, first)
            pconv = sb("pconv", [P, 2, T], F32, first)
            prod = sb("prod", [P, 3, T], F32, first)
        wo_hi = sb("wo_hi", [P, KC, D], F32R)
        wo_lo = sb("wo_lo", [P, KC, D], F32R)
        act_v = sb("act_v", [P, NH, HALF])

        acc = ctx.enter_context(nc.psum_tensor("acc", [P, 4, HALF], F32))
        mm = ctx.enter_context(nc.psum_tensor("mm", [P, 4, HALF], F32))
        acc2 = [acc[:, 0:2, :].rearrange("p a b -> p (a b)"), acc[:, 2:4, :].rearrange("p a b -> p (a b)")]

        consts_in = sem("consts_in")
        x_in = [sem(f"x_in{t}") for t in range(NT)]
        raw_in = [sem(f"raw_in{i}") for i in range(2)]
        sumsq_ready = [sem(f"sumsq_ready{t}") for t in range(NT)]
        exponent_ready = sem("exponent_ready")
        pads_ready = sem("pads_ready")
        ms_ready = sem("ms_ready")
        rms_ready = sem("rms_ready")
        xs_ready = [sem(f"xs_ready{t}") for t in range(NT)]
        xt_ready = sem("xt_ready")
        xhi_ready = sem("xhi_ready")
        xlo_ready = sem("xlo_ready")
        whi_ready = sem("whi_ready")
        wlo_ready = sem("wlo_ready")
        unit_ready = {k: sem(f"{k}_ready") for k in "abg"}
        bank_free = [sem(f"bank_free{i}") for i in range(4)]
        x1_free = sem("x1_free")
        sig_ready = sem("sig_ready")
        u_ready = sem("u_ready")
        sgate_ready = sem("sgate_ready")
        steps_done = sem("steps_done")
        prod_ready = sem("prod_ready")
        sums_done = sem("sums_done")
        ct_ready = sem("ct_ready")
        ct_copied = sem("ct_copied")
        stats_ready = sem("stats_ready")
        mv_ready = sem("mv_ready")
        veps_ready = sem("veps_ready")
        rstd_ready = sem("rstd_ready")
        shift_ready = sem("shift_ready")
        norm_dve = sem("norm_dve")
        norm_act = sem("norm_act")
        nt_ready = sem("nt_ready")
        actv_ready = sem("actv_ready")
        v_ready = sem("v_ready")
        vhi_ready = sem("vhi_ready")
        vlo_ready = sem("vlo_ready")
        y_ready = sem("y_ready")
        y_added = sem("y_added")
        y_out = sem("y_out")

        JOBS = [("x", 0, k) for k in range(KC)]
        JOBS += [("unit", 0, 0), ("unit", 1, 0), ("unit", 0, 1), ("unit", 1, 1)]
        for m in range(2, NU):
            JOBS += [("unit", m, 0), ("unit", m, 1)]
            JOBS += [("conv", j, h) for j in TRANSPOSE_AFTER.get(m, []) for h in range(NH)]
        JOBS += [("norm", k, h) for k in range(KC) for h in range(NH)]
        NUMBER = {job: n for n, job in enumerate(JOBS)}
        CONV_ORDER = [j for kind, j, h in JOBS if kind == "conv" and h == 0]

        def bank(job):
            if job[:2] == ("x", 1):
                return acc[:, job[2] % 4, :]
            return mm[:, NUMBER[job] % 4, :]

        def free(job):
            if job[:2] == ("x", 1):
                return x1_free
            return bank_free[NUMBER[job] % 4]

        def wait_bank(pe, job):
            if job[:2] == ("x", 1):
                if job[2] >= 4:
                    pe.wait_ge(x1_free, job[2] - 3)
                return
            n = NUMBER[job]
            if n >= 4:
                pe.wait_ge(bank_free[n % 4], n // 4)

        def nth(kind, m):
            return sum(k == kind for k, _ in UNITS[:m + 1])

        def pool_slot(j):
            return [i for i, _ in POOL_PARTS].index(j) % 2

        def u_in(j, k):
            return u[:, j % 4, k:k + T]

        def terms(hi1, lo1, hi2, lo2):
            return ((hi1, hi2), (hi1, lo2), (lo1, hi2))

        block = ctx.enter_context(nc.Block())

        @block.sync
        def _(sp):
            for t in range(NT):
                if t == 5:
                    sp.dma_start(raw[:, 0, :], w_in[PART[UNITS[0][0]], UNITS[0][1]]).then_inc(raw_in[0], 16)
                sp.dma_start(nat[:, t, :], x[t * P:(t + 1) * P, :]).then_inc(x_in[t], 16)
            for m in range(1, NU):
                kind, j = UNITS[m]
                if m >= 2:
                    sp.wait_ge(wlo_ready, m - 1)
                sp.dma_start(raw[:, m % 2, :], w_in[PART[kind], j]).then_inc(raw_in[m % 2], 16)
            for r in range(NWO):
                m = NU + r
                sp.wait_ge(wlo_ready, m - 1)
                sp.dma_start(raw[:, m % 2, :].rearrange("p (k n) -> p k n", k=2),
                             w_out[r // (KC // 2), r % (KC // 2)]).then_inc(raw_in[m % 2], 16)
            sp.wait_ge(nt_ready, KC * NH)
            for t in range(NT):
                sp.dma_start(nat[:, t, :], x[t * P:(t + 1) * P, :]).then_inc(x_in[t], 16)
            for q in range(NH * NT):
                n, t = divmod(q, NT)
                sp.wait_ge(y_added, q + 1)
                sp.dma_start(out[t * P:(t + 1) * P, n * HALF:(n + 1) * HALF],
                             nat[:, t, n * HALF:(n + 1) * HALF]).then_inc(y_out, 16)
            sp.wait_ge(y_out, 16 * NH * NT)

        @block.tensor
        def _(pe):
            def transpose_x(h, k):
                wait_bank(pe, ("x", h, k))
                for i in range(TPH):
                    t = TPH * h + i
                    pe.wait_ge(xs_ready[t], 1)
                    ins = nc.tensor.transpose(bank(("x", h, k))[:, i * P:(i + 1) * P],
                                              nat[:, t, k * P:(k + 1) * P], ident[:])
                ins.then_inc(xt_ready, 1)

            def project(m, h):
                kind, _ = UNITS[m]
                pe.wait_ge(wlo_ready, m + 1)
                wait_bank(pe, ("unit", m, h))
                for k in range(KC):
                    if m == 0:
                        pe.wait_ge(xlo_ready, KC * h + k + 1)
                    for i, (w, xx) in enumerate(terms(w_hi, w_lo, x_hi, x_lo)):
                        ins = nc.tensor.matmul(bank(("unit", m, h)), w[:, m % 3, k, :],
                                               xx[:, k, h * HALF:(h + 1) * HALF],
                                               start=(k == 0 and i == 0), stop=(k == KC - 1 and i == 2))
                ins.then_inc(unit_ready[kind], 1)

            def transpose_conv(j, h):
                wait_bank(pe, ("conv", j, h))
                if j in STEP_END:
                    pe.wait_ge(steps_done, STEP_END[j])
                    src = dconv[:, :]
                else:
                    pe.wait_ge(sums_done, SUM_END[j])
                    src = pconv[:, pool_slot(j), :]
                for i in range(TPH):
                    t = TPH * h + i
                    ins = nc.tensor.transpose(bank(("conv", j, h))[:, i * P:(i + 1) * P],
                                              src[:, t * P:(t + 1) * P], ident[:])
                ins.then_inc(ct_ready, 1)

            def transpose_norm(k, h):
                wait_bank(pe, ("norm", k, h))
                pe.wait_ge(norm_dve, NT // 2)
                pe.wait_ge(norm_act, NT // 2)
                for i in range(TPH):
                    t = TPH * h + i
                    ins = nc.tensor.transpose(bank(("norm", k, h))[:, i * P:(i + 1) * P],
                                              nat[:, t, k * P:(k + 1) * P], ident[:])
                ins.then_inc(nt_ready, 1)

            def out_product(dst, t, n, k):
                for i, (v, w) in enumerate(terms(x_hi, x_lo, wo_hi, wo_lo)):
                    ins = nc.tensor.matmul(dst, v[:, k, t * P:(t + 1) * P], w[:, k, n * HALF:(n + 1) * HALF],
                                           start=(k == 0 and i == 0), stop=(k == KC - 1 and i == 2))
                return ins

            pe.wait_ge(consts_in, 32)
            for k in range(KC):
                transpose_x(0, k)
            for k in range(KC // 2):
                transpose_x(1, k)
            project(0, 0)
            for k in range(KC // 2, KC):
                transpose_x(1, k)
            project(1, 0)
            for m in range(2):
                project(m, 1)
            for m in range(2, NU):
                project(m, 0)
                project(m, 1)
                for j in TRANSPOSE_AFTER.get(m, []):
                    for h in range(NH):
                        transpose_conv(j, h)

            for k in range(KC + AHEAD):
                if k < KC:
                    for h in range(NH):
                        transpose_norm(k, h)
                if k >= AHEAD:
                    pe.wait_ge(vlo_ready, k - AHEAD + 1)
                    pe.wait_ge(wlo_ready, NU + (k - AHEAD) // 2 + 1)
                    for t in range(4):
                        ins = out_product(acc[:, t, :], t, 0, k - AHEAD)
                        if k == KC + AHEAD - 1:
                            ins.then_inc(y_ready, 1)
            for q in range(4, NH * NT):
                n, t = divmod(q, NT)
                if q == NT:
                    pe.wait_ge(wlo_ready, NU + NWO)
                if q < 8:
                    last = ("norm", KC - 1, 0)
                    uses = sum(i % 4 == q % 4 for i in range(len(JOBS)))
                    pe.wait_ge(bank_free[q % 4], uses)
                else:
                    pe.wait_ge(y_added, q - 7)
                dst = (acc if q % 8 < 4 else mm)[:, q % 4, :]
                for k in range(KC):
                    ins = out_product(dst, t, n, k)
                ins.then_inc(y_ready, 1)

        @block.scalar
        def _(act):
            act.dma_start(chan[:], per_channel).then_inc(consts_in, 16)
            act.dma_start(ident[:], identity).then_inc(consts_in, 16)

            def square(t):
                act.wait_ge(x_in[t], 16)
                nc.scalar.activation(sgate[:, t, :], nat[:, t, :], ACT.Square,
                                     accum_out=sumsq[:, t:t + 1]).then_inc(sumsq_ready[t], 1)

            def split_x(h, k):
                act.wait_ge(xt_ready, KC * h + k + 1)
                nc.scalar.activation(x_hi[:, k, h * HALF:(h + 1) * HALF], bank(("x", h, k)), ACT.Copy,
                                     scale=norm_g[:, k:k + 1]).then_inc(xhi_ready, 1)

            def split_w(m):
                act.wait_ge(raw_in[m % 2], 16 * (m // 2 + 1))
                if m >= 3:
                    count_used(m - 3)
                nc.scalar.activation(w_hi[:, m % 3, :, :].rearrange("p k n -> p (k n)"), raw[:, m % 2, :],
                                     ACT.Copy).then_inc(whi_ready, 1)

            def count_used(m):
                kind, _ = UNITS[m]
                act.wait_ge(unit_ready[kind], NH * nth(kind, m))

            def read_unit(m, h):
                kind, j = UNITS[m]
                act.wait_ge(unit_ready[kind], NH * (nth(kind, m) - 1) + h + 1)
                if kind == "b":
                    if j >= 1:
                        act.wait_ge(u_ready, NH * (j - 1) + h + 1)
                    nc.scalar.activation(sig[:, h, :], bank(("unit", m, h)), ACT.Sigmoid).then_inc(sig_ready, 1)
                    act.wait_ge(sig_ready, NH * j + h + 1)
                    act.sem_inc(free(("unit", m, h)), 1)
                else:
                    nc.scalar.activation(sgate[:, j, h * HALF:(h + 1) * HALF], bank(("unit", m, h)),
                                         ACT.Silu).then_inc(free(("unit", m, h)), 1)

            def product(n):
                j, k = PRODUCTS[n]
                if k == 0:
                    act.wait_ge(u_ready, NH * (j + 1))
                if n >= 3:
                    j0, k0 = PRODUCTS[n - 3]
                    act.wait_ge(sums_done, SUM_END[j0] - (POOL_TAPS[j0] - 1) + max(k0, 1))
                nc.scalar.activation(prod[:, n % 3, :], u_in(j, k), ACT.Identity, scale=conv_w[:, j, k:k + 1],
                                     bias=conv_b[:, j:j + 1] if k == 0 else 0.0).then_inc(prod_ready, 1)

            def copy_conv(j, h):
                i = NH * CONV_ORDER.index(j) + h
                act.wait_ge(ct_ready, i + 1)
                nc.scalar.activation(nat[:, TPH * h:TPH * (h + 1), j * P:(j + 1) * P],
                                     bank(("conv", j, h)).rearrange("p (t c) -> p t c", c=P),
                                     ACT.Copy).then_inc(ct_copied, 1)
                act.wait_ge(ct_copied, i + 1)
                act.sem_inc(free(("conv", j, h)), 1)

            for t in (0, 2, 4):
                square(t)
            split_w(0)
            for k in range(KC):
                split_x(0, k)
                if k in (1, 4):
                    square(6 + k // 4)
            split_w(1)
            for k in range(KC):
                if k == 4:
                    read_unit(0, 0)
                split_x(1, k)

            made = 0
            for m in range(NU):
                if m + 2 < NU:
                    split_w(m + 2)
                for j in TRANSPOSE_AFTER.get(m - 1, []):
                    for h in range(NH):
                        copy_conv(j, h)
                quota = products_by[m]
                middle = (made + quota) // 2
                while made < middle:
                    product(made)
                    made += 1
                if UNITS[m][0] != "a" and m > 0:
                    read_unit(m, 0)
                while made < quota:
                    product(made)
                    made += 1
                if UNITS[m][0] != "a":
                    read_unit(m, 1)
            while made < len(PRODUCTS):
                product(made)
                made += 1
            for j in TRANSPOSE_AFTER[NU - 1]:
                for h in range(NH):
                    copy_conv(j, h)

            def split_wo(r):
                m = NU + r
                n, kp = divmod(r, KC // 2)
                act.wait_ge(raw_in[m % 2], 16 * (m // 2 + 1))
                nc.scalar.activation(wo_hi[:, 2 * kp:2 * kp + 2, n * HALF:(n + 1) * HALF],
                                     raw[:, m % 2, :].rearrange("p (k n) -> p k n", k=2),
                                     ACT.Copy).then_inc(whi_ready, 1)

            count_used(NU - 1)
            act.wait_ge(prod_ready, len(PRODUCTS))
            act.wait_ge(steps_done, len(STEPS))
            act.wait_ge(ct_ready, NH * KC)
            act.wait_ge(u_ready, NH * KC)
            for r in range(2):
                split_wo(r)
            act.wait_ge(shift_ready, 1)
            for t in range(NT // 2, NT):
                nc.scalar.activation(nat[:, t, :], nat[:, t, :], ACT.Identity, scale=rstd[:, t:t + 1],
                                     bias=shift[:, t:t + 1]).then_inc(norm_act, 1)

            def act_norm(k, h):
                act.wait_ge(nt_ready, NH * k + h + 1)
                if k >= 1:
                    act.wait_ge(v_ready, NH * (k - 1) + h + 1)
                nc.scalar.activation(act_v[:, h, :], bank(("norm", k, h)), ACT.Silu, scale=ln_g[:, k:k + 1],
                                     bias=ln_b[:, k:k + 1]).then_inc(actv_ready, 1)
                act.wait_ge(actv_ready, NH * k + h + 1)
                act.sem_inc(free(("norm", k, h)), 1)

            for k in range(KC + 1):
                if k < KC:
                    for h in range(NH):
                        act_norm(k, h)
                if k > 0:
                    act.wait_ge(v_ready, NH * k)
                    nc.scalar.activation(x_hi[:, k - 1, :], sgate[:, k - 1, :], ACT.Copy).then_inc(vhi_ready, 1)
                if k < NWO - 2:
                    split_wo(k + 2)

        @block.vector
        def _(dve):
            nc.vector.memset(half_neg[:], -0.5).then_inc(exponent_ready, 1)
            nc.vector.memset(u[:, :, 0:PAD], 0.0).then_inc(pads_ready, 1)
            dve.wait_ge(pads_ready, 1)

            def square(t):
                dve.wait_ge(x_in[t], 16)
                nc.vector.tensor_tensor_reduce(out=sgate[:, t, :], in0=nat[:, t, :], in1=nat[:, t, :], scale=1.0,
                                               scalar=0.0, op0=ALU.mult, op1=ALU.add,
                                               accum_out=sumsq[:, t:t + 1]).then_inc(sumsq_ready[t], 1)

            def scale_x(t):
                dve.wait_ge(rms_ready, t + 1)
                nc.vector.tensor_scalar(nat[:, t, :], nat[:, t, :], rms[:, t:t + 1], None,
                                        ALU.mult).then_inc(xs_ready[t], 1)

            def split_x(h, k):
                dve.wait_ge(xhi_ready, KC * h + k + 1)
                part = slice(h * HALF, (h + 1) * HALF)
                nc.vector.scalar_tensor_tensor(x_lo[:, k, part], bank(("x", h, k)), norm_g[:, k:k + 1],
                                               x_hi[:, k, part].bitcast(F32), ALU.mult,
                                               ALU.subtract).then_inc(xlo_ready, 1)
                dve.wait_ge(xlo_ready, KC * h + k + 1)
                dve.sem_inc(free(("x", h, k)), 1)

            def split_w(m):
                dve.wait_ge(whi_ready, m + 1)
                nc.vector.tensor_tensor(w_lo[:, m % 3, :, :].rearrange("p k n -> p (k n)"), raw[:, m % 2, :],
                                        w_hi[:, m % 3, :, :].rearrange("p k n -> p (k n)").bitcast(F32),
                                        ALU.subtract).then_inc(wlo_ready, 1)

            def conv_in(m, h):
                _, j = UNITS[m]
                dve.wait_ge(unit_ready["a"], NH * j + h + 1)
                dve.wait_ge(sig_ready, NH * j + h + 1)
                if j >= 4:
                    if j - 4 in STEP_END:
                        dve.wait_ge(steps_done, STEP_END[j - 4])
                    if j - 4 in PRODUCT_END:
                        dve.wait_ge(prod_ready, PRODUCT_END[j - 4])
                nc.vector.tensor_tensor(u[:, j % 4, PAD + h * HALF:PAD + (h + 1) * HALF], bank(("unit", m, h)),
                                        sig[:, h, :], ALU.mult).then_inc(u_ready, 1)
                dve.wait_ge(u_ready, NH * j + h + 1)
                dve.sem_inc(free(("unit", m, h)), 1)

            def step(n):
                j, k = STEPS[n]
                begin = POOL_TAPS.get(j, 0)
                if k in ("join", "pool"):
                    dve.wait_ge(steps_done, n)
                    other = acc2[(TAPS - 1) % 2]
                    if k == "pool":
                        dve.wait_ge(sums_done, SUM_END[j])
                        other = pconv[:, pool_slot(j), :]
                    nc.vector.tensor_tensor(dconv[:, :], other, dconv[:, :], ALU.add).then_inc(steps_done, 1)
                    return
                if k == begin:
                    dve.wait_ge(u_ready, NH * (j + 1))
                if n == 0:
                    dve.wait_ge(x1_free, KC)
                if n >= 2:
                    dve.wait_ge(steps_done, n if k == begin else n - 1)
                w = conv_w[:, j, k:k + 1]
                if k == 0:
                    ins = nc.vector.tensor_scalar(acc2[0], u_in(j, k), w, conv_b[:, j:j + 1], ALU.mult, ALU.add)
                elif k < begin + 2:
                    ins = nc.vector.tensor_scalar(acc2[k % 2], u_in(j, k), w, None, ALU.mult)
                else:
                    dst = acc2[k % 2]
                    if k == TAPS - 2:
                        dst = dconv[:, :]
                        before = [i for i in VECTOR_TILES if STEP_END[i] < STEP_END[j]]
                        if before:
                            dve.wait_ge(ct_ready, NH * (CONV_ORDER.index(before[-1]) + 1))
                    ins = nc.vector.scalar_tensor_tensor(dst, u_in(j, k), w, acc2[k % 2], ALU.mult, ALU.add)
                ins.then_inc(steps_done, 1)

            def split_wo(r):
                m = NU + r
                n, kp = divmod(r, KC // 2)
                dve.wait_ge(whi_ready, m + 1)
                part = (slice(None), slice(2 * kp, 2 * kp + 2), slice(n * HALF, (n + 1) * HALF))
                nc.vector.tensor_tensor(wo_lo[part], raw[:, m % 2, :].rearrange("p (k n) -> p k n", k=2),
                                        wo_hi[part].bitcast(F32), ALU.subtract).then_inc(wlo_ready, 1)

            def take_stats(g):
                need = max(CONV_ORDER.index(2 * g), CONV_ORDER.index(2 * g + 1)) + 1
                dve.wait_ge(ct_copied, NH * need)
                for t in range(NT):
                    nc.vector.bn_stats(stats[:, t, g, :], nat[:, t, 2 * g * P:2 * (g + 1) * P]).then_inc(stats_ready, 1)

            square(1)
            scale_x(0)
            scale_x(1)
            square(3)
            scale_x(2)
            scale_x(3)
            square(5)
            for k in range(KC):
                split_x(0, k)
                if k == 3:
                    split_w(0)
                    scale_x(4)
            split_w(1)
            for k in range(KC):
                split_x(1, k)
            conv_in(1, 0)

            total = len(STEPS)
            done = 0
            for m in range(NU):
                if m + 2 < NU:
                    split_w(m + 2)
                quota = steps_by[m]
                middle = (done + quota) // 2
                if m > 0 and UNITS[m - 1][0] == "a":
                    if done < quota and UNITS.index(("a", STEPS[done][0])) < m - 1:
                        step(done)
                        done += 1
                    conv_in(m - 1, 1)
                while done < middle:
                    step(done)
                    done += 1
                if UNITS[m][0] == "a" and m > 1:
                    conv_in(m, 0)
                while done < quota:
                    step(done)
                    done += 1
                for g in STATS_AFTER.get(m, []):
                    take_stats(g)
            while done < total:
                step(done)
                done += 1
            for r in range(2):
                split_wo(r)
            for g in STATS_AFTER.get(NU, []):
                take_stats(g)
            dve.wait_ge(stats_ready, NT * KC // 2)
            for t in range(NT):
                nc.vector.bn_aggr(mean_var[:, t, :], stats[:, t, :, :].rearrange("p g s -> p (g s)")).then_inc(mv_ready, 1)

            dve.wait_ge(rstd_ready, 1)
            nc.vector.scalar_tensor_tensor(shift[:], mean_var[:, :, 0], -1.0, rstd[:], ALU.mult,
                                           ALU.mult).then_inc(shift_ready, 1)
            for t in range(NT // 2):
                nc.vector.tensor_scalar(nat[:, t, :], nat[:, t, :], mean_var[:, t, 0:1], rstd[:, t:t + 1],
                                        ALU.subtract, ALU.mult).then_inc(norm_dve, 1)

            for k in range(KC + 1):
                if k < KC:
                    for h in range(NH):
                        part = slice(h * HALF, (h + 1) * HALF)
                        dve.wait_ge(actv_ready, NH * k + h + 1)
                        dve.wait_ge(free(("unit", UNITS.index(("g", k)), h)),
                                    NUMBER[("unit", UNITS.index(("g", k)), h)] // 4 + 1)
                        nc.vector.tensor_tensor(sgate[:, k, part], act_v[:, h, :], sgate[:, k, part],
                                                ALU.mult).then_inc(v_ready, 1)
                if k > 0:
                    dve.wait_ge(vhi_ready, k)
                    nc.vector.tensor_tensor(x_lo[:, k - 1, :], sgate[:, k - 1, :], x_hi[:, k - 1, :].bitcast(F32),
                                            ALU.subtract).then_inc(vlo_ready, 1)
                if k < NWO - 2:
                    split_wo(k + 2)

            for q in range(NH * NT):
                n, t = divmod(q, NT)
                if n == 0:
                    dve.wait_ge(x_in[t], 32)
                dve.wait_ge(y_ready, q + 1)
                part = (slice(None), t, slice(n * HALF, (n + 1) * HALF))
                src = (acc if q % 8 < 4 else mm)[:, q % 4, :]
                nc.vector.tensor_tensor(nat[part], src, nat[part], ALU.add).then_inc(y_added, 1)

        @block.gpsimd
        def _(pool):
            pool.wait_ge(exponent_ready, 1)
            for t in range(NT):
                part = slice(t, t + 1)
                pool.wait_ge(sumsq_ready[t], 1)
                nc.gpsimd.tensor_scalar(sumsq[:, part], sumsq[:, part], 1.0 / D, RMS_EPS, ALU.mult,
                                        ALU.add).then_inc(ms_ready, 1)
                pool.wait_ge(ms_ready, t + 1)
                nc.gpsimd.tensor_tensor(rms[:, part], sumsq[:, part], half_neg[:, part],
                                        ALU.pow).then_inc(rms_ready, 1)
                if t > 4:
                    pool.wait_ge(rms_ready, t + 1)
                    nc.gpsimd.tensor_scalar(nat[:, t, :], nat[:, t, :], rms[:, t:t + 1], 0.0, ALU.mult,
                                            ALU.add).then_inc(xs_ready[t], 1)

            n = 0
            for i, (j, count) in enumerate(POOL_PARTS):
                dst = pconv[:, i % 2, :]
                if i >= 2:
                    j0 = POOL_PARTS[i - 2][0]
                    if j0 in STEP_END:
                        pool.wait_ge(steps_done, STEP_END[j0])
                    else:
                        pool.wait_ge(ct_ready, NH * (CONV_ORDER.index(j0) + 1))
                for k in range(1, count):
                    p = PRODUCTS.index((j, k))
                    pool.wait_ge(prod_ready, p + 1)
                    if k > 1:
                        pool.wait_ge(sums_done, n)
                    nc.gpsimd.tensor_tensor(dst, prod[:, (p - 1) % 3, :] if k == 1 else dst, prod[:, p % 3, :],
                                            ALU.add).then_inc(sums_done, 1)
                    n += 1

            pool.wait_ge(mv_ready, NT)
            nc.gpsimd.tensor_scalar(var_eps[:], mean_var[:, :, 1], 1.0, LN_EPS, ALU.mult,
                                    ALU.add).then_inc(veps_ready, 1)
            pool.wait_ge(veps_ready, 1)
            nc.gpsimd.tensor_tensor(rstd[:], var_eps[:], half_neg[:], ALU.pow).then_inc(rstd_ready, 1)


def kernel(**inputs):
    import numpy as np
    import concourse.bacc as bacc
    from concourse.bass_utils import run_bass_kernel_spmd

    def arr(name):
        return np.asarray(inputs[name])

    x = arr("x")[0]
    T, D = x.shape
    KC = D // P
    w_in, w_out = arr("a_w_in")[0], arr("a_w_out")[0]
    conv_w = arr("a_conv_w")[0]
    w_in = w_in.reshape(KC, P, 3, KC, P).transpose(2, 3, 1, 0, 4).reshape(3, KC, P, KC * P)
    w_out = w_out.reshape(KC // 2, 2, P, D // HALF, HALF).transpose(3, 0, 2, 1, 4)

    def by_channel(v):
        return v.reshape(KC, P).T

    per_channel = np.concatenate(
        [conv_w.reshape(-1, KC, P).transpose(2, 1, 0).reshape(P, -1)]
        + [by_channel(arr(n)[0]) for n in ("a_conv_b", "a_ln_g", "a_ln_b", "norm_g")], axis=1)
    arrays = {k: np.ascontiguousarray(v) for k, v in {
        "x": x, "w_in": w_in, "w_out": w_out, "per_channel": per_channel,
        "identity": np.eye(P, dtype=np.float32)}.items()}

    nc = bacc.Bacc("TRN2", target_bir_lowering=False, num_devices=1)
    aps = [nc.dram_tensor(k, v.shape, F32, kind="ExternalInput").ap() for k, v in arrays.items()]
    out = nc.dram_tensor("y", [T, D], F32, kind="ExternalOutput").ap()
    gated_conv_layer(nc, *aps, out)
    r = run_bass_kernel_spmd(nc, [arrays], core_ids=[0])
    return r.results[0]["y"].reshape(1, T, D)
```

```python
from contextlib import ExitStack

import concourse.bass as bass
from concourse import mybir

F32 = mybir.dt.float32
F32R = mybir.dt.float32r
ALU = mybir.AluOpType
ACT = mybir.ActivationFunctionType

P = 128
HALF = 512
RMS_EPS = 1e-6
LN_EPS = 1e-5

STAGES = [("ab", 0), ("ab", 1), ("ab", 2), ("ab", 3), ("ab", 4), ("g", 0), ("ab", 5), ("g", 1),
          ("ab", 6), ("g", 2), ("ab", 7), ("g", 3), ("g", 4), ("g", 5), ("g", 6), ("g", 7)]

TAPS0, TAPS1, TAPS6 = 13, 20, 26
GPSIMD_PARTS = [(0, (0,), range(0, TAPS0)), (0, (1,), range(0, TAPS0)), (1, (0, 1), range(0, TAPS1)),
                (3, (0, 1), range(0, 31)), (6, (0,), range(0, 31)), (6, (1,), range(0, TAPS6))]
VECTOR_PARTS = [(0, (0,), range(TAPS0, 31)), (0, (1,), range(TAPS0, 31)), (1, (0, 1), range(TAPS1, 31)),
                (2, (0, 1), range(0, 31)), (4, (0, 1), range(0, 31)), (5, (0, 1), range(0, 31)),
                (7, (0,), range(0, 31)), (7, (1,), range(0, 31)), (6, (1,), range(TAPS6, 31))]
JOINS = {0: 3, 1: 20}
LATE = [(7, 1), (6, 1)]

UNIT_US, SPLIT_US, CONV_IN_US, STEP_US, SUM_US = 10.45, 1.2, 0.75, (0.67, 1.18), (1.25, 2.38)
SUM_ROOM, FIRST_ROOM, CARRY = 10.2, 12, 1.0
DELAYED = (0, 1, 2, 3, 4)

LAG = 3
LO_BY_POOL = (3, 5, 7)
SQUARE_AT = [5, 6, 7, 7]
POW_AT = [6, 7, 7, 7]
DIAG_AT, SPREAD_AT = 7, 5
SIGMOID_AT, CONV_IN_AT = 3, 5

STEPS_BEFORE_MOMENTS, STEPS_BEFORE_NORM, STEPS_AFTER_NORM = 0, 2, 4
RSTD_TAP = 18
NORM_AT = 5
LATE_AT = 3
SPLIT_WITH = {1: 1, 2: 2, 3: 4, 4: 6, 5: 7}
STREAM_STEPS, STREAM_PRODUCTS = 2, 5


def gated_conv_layer(nc, x, x_t, w_in, w_out, per_channel, identity, out):
    T, D = x.shape
    NT, KC = T // P, D // P
    TAPS = per_channel.shape[1] // KC - 4
    PAD = TAPS - 1
    NH = T // HALF
    TPH = HALF // P
    UNITS = [m for kind, j in STAGES for m in ([("b", j), ("a", j)] if kind == "ab" else [("g", j)])]
    NU = len(UNITS)
    PART = {"a": 0, "b": 1, "g": 2}
    AHEAD = 2

    STEPS = [(j, halves, k) for j, halves, taps in VECTOR_PARTS for k in [*taps, "join"]]
    STEPS[-1:] = [(6, (1,), "even"), (6, (1,), "odd")]
    for j, at in JOINS.items():
        STEPS.insert([n for n, (i, _, _) in enumerate(STEPS) if i == j + 1][at], (j, (0, 1), "gpsimd"))
    FIRST_TAP = {(j, h): taps[0] for j, halves, taps in VECTOR_PARTS for h in halves}
    STEP_END = {(j, h): n + 1 for n, (j, halves, _) in enumerate(STEPS) for h in halves}
    VECTOR_TILES = [j for j, halves, _ in VECTOR_PARTS if 0 in halves]
    GPSIMD_TILES = sorted({j for j, _, _ in GPSIMD_PARTS})
    PRODUCTS = [(j, halves, k) for j, halves, taps in GPSIMD_PARTS for k in taps]
    PRODUCT_END = {(j, h): n + 1 for n, (j, halves, _) in enumerate(PRODUCTS) for h in halves}
    SUM_OF, SUM_END = [], {}
    for i, (j, halves, taps) in enumerate(GPSIMD_PARTS):
        base = len(SUM_OF) - i
        SUM_OF += [base + max(k, 1) for k in taps]
        SUM_END.update({(j, h): SUM_OF[-1] for h in halves})

    def by_unit(work, room, cost, ready=lambda n, m, counts: True):
        counts, n, rest = [], 0, 0.0
        for m in range(NU):
            rest += room(m)
            while n < len(work):
                j, halves, _ = work[n]
                us = cost[len(halves) - 1]
                early = j == 0 and halves == (0,)
                if rest < us or not (early or UNITS.index(("a", j)) < m) or not ready(n, m, counts):
                    break
                n, rest = n + 1, rest - us
            rest = min(rest, CARRY)
            counts.append(n)
        return counts

    def step_room(m):
        us = UNIT_US if m > 1 else FIRST_ROOM if m == 0 else UNIT_US / 2
        us -= SPLIT_US * (m + 2 < NU)
        return us - CONV_IN_US * ((UNITS[m][0] == "a") + (m > 0 and UNITS[m - 1][0] == "a"))

    steps_by = by_unit(STEPS, step_room, STEP_US)

    def buffer_free(n, m, counts):
        j, halves, k = PRODUCTS[n]
        i = GPSIMD_TILES.index(j)
        if i < 2 or k < 3:
            return True
        held = (GPSIMD_TILES[i - 2], halves[-1])
        if held in STEP_END:
            return steps_by[m - 2] >= STEP_END[held]
        return counts[m - 3] >= PRODUCT_END[held]

    products_by = by_unit(PRODUCTS, lambda m: SUM_ROOM, SUM_US, buffer_free)

    TRANSPOSE_AFTER = {}
    for j in range(KC):
        for h in range(NH):
            if (j, h) in LATE:
                continue
            m = 0
            while m < NU - 1 and (((j, h) in STEP_END and steps_by[m] < STEP_END[j, h])
                                  or ((j, h) not in STEP_END
                                      and products_by[max(m - 1, 0)] < PRODUCT_END[j, h])):
                m += 1
            if j in DELAYED:
                m += 1
            TRANSPOSE_AFTER.setdefault(m, []).append((j, h))
    AFTER = {jh: m for m, tiles in TRANSPOSE_AFTER.items() for jh in tiles}
    STATS_AFTER = {}
    for g in range(KC // 2 - 1):
        last = max(AFTER[j, h] for j in (2 * g, 2 * g + 1) for h in range(NH))
        assert last < NU - 1
        STATS_AFTER.setdefault(min(NU, last + 1), []).append(g)
    NWO = NH * KC // 2

    ctx = ExitStack()
    with ctx:
        def sb(name, shape, dt=F32, into=ctx):
            return into.enter_context(nc.sbuf_tensor(name, shape, dt))

        def sem(name):
            return ctx.enter_context(nc.semaphore(name))

        nat = sb("nat", [P, NT, D])
        x_hi = sb("x_hi", [P, KC, T], F32R)
        x_lo = sb("x_lo", [P, KC, T], F32R)
        sgate = sb("sgate", [P, KC, T])
        raw = sb("raw", [P, 2, KC * P])
        chan = sb("chan", [P, KC * (TAPS + 4)])
        ident = sb("ident", [P, P])
        ones = sb("ones", [P, P])
        mean_sq = sb("mean_sq", [P, NT])
        rms = sb("rms", [P, NT])
        half_neg = sb("half_neg", [P, NT])
        stats = sb("stats", [P, NT, KC // 2, 6])
        mean_var = sb("mean_var", [P, NT, 2])
        var_eps = sb("var_eps", [P, NT])
        rstd = sb("rstd", [P, NT])
        shift = sb("shift", [P, NT])
        conv_w = chan[:, 0:KC * TAPS].rearrange("p (j k) -> p j k", k=TAPS)
        conv_b, ln_g, ln_b, norm_g = (
            chan[:, KC * (TAPS + i):KC * (TAPS + i + 1)] for i in range(4))

        sig = sb("sig", [P, 2, HALF])

        first = ExitStack()
        with first:
            w_hi = sb("w_hi", [P, 3, KC, P], F32R, first)
            w_lo = sb("w_lo", [P, 3, KC, P], F32R, first)
            u = sb("u", [P, 4, PAD + T], F32, first)
            dconv = sb("dconv", [P, T], F32, first)
            pconv = sb("pconv", [P, 2, T], F32, first)
            prod = sb("prod", [P, 3, T], F32, first)
        wo = {}
        for n, kp in [(0, 0), (0, 1), (0, 2), (0, 3), (1, 2), (1, 3), (1, 0), (1, 1)]:
            if (n, kp) == (1, 0):
                sb("space", [P, 4 * PAD])
            wo[n, kp] = [sb(f"wo_{part}{n}{kp}", [P, 2, HALF], F32R) for part in ("hi", "lo")]

        acc = ctx.enter_context(nc.psum_tensor("acc", [P, 4, HALF], F32))
        mm = ctx.enter_context(nc.psum_tensor("mm", [P, 4, HALF], F32))

        consts_in = sem("consts_in")
        xt_in = [[sem(f"xt_in{h}{k}") for k in range(KC)] for h in range(NH)]
        x_in = [sem(f"x_in{t}") for t in range(NT)]
        raw_in = [sem(f"raw_in{i}") for i in range(2)]
        x_sq_in = [sem(f"x_sq_in{t}") for t in range(NT)]
        sumsq_ready = sem("sumsq_ready")
        ones_ready = sem("ones_ready")
        diag_ready = sem("diag_ready")
        rms_all_ready = sem("rms_all_ready")
        hn_ready = sem("hn_ready")
        xlo_pool = sem("xlo_pool")
        exponent_ready = sem("exponent_ready")
        pads_ready = sem("pads_ready")
        ms_ready = sem("ms_ready")
        rms_ready = sem("rms_ready")
        xhi_ready = sem("xhi_ready")
        xlo_ready = sem("xlo_ready")
        whi_ready = sem("whi_ready")
        wlo_ready = sem("wlo_ready")
        unit_ready = {k: sem(f"{k}_ready") for k in "abg"}
        bank_free = [sem(f"bank_free{i}") for i in range(4)]
        sig_ready = sem("sig_ready")
        u_ready = sem("u_ready")
        steps_done = sem("steps_done")
        prod_ready = sem("prod_ready")
        sums_done = sem("sums_done")
        ct_ready = sem("ct_ready")
        ct_copied = sem("ct_copied")
        stats_ready = sem("stats_ready")
        mv_ready = sem("mv_ready")
        veps_ready = sem("veps_ready")
        rstd_ready = sem("rstd_ready")
        shift_ready = sem("shift_ready")
        norm_dve = sem("norm_dve")
        norm_act = sem("norm_act")
        nt_ready = sem("nt_ready")
        actv_ready = sem("actv_ready")
        v_ready = sem("v_ready")
        vhi_ready = sem("vhi_ready")
        vlo_ready = sem("vlo_ready")
        y_ready = sem("y_ready")
        y_added = sem("y_added")
        y_out = sem("y_out")

        JOBS = [("unit", 0, 0), ("unit", 1, 0), ("unit", 0, 1), ("unit", 1, 1)]
        for m in range(2, NU):
            JOBS += [("unit", m, 0), ("unit", m, 1)]
            JOBS += [("conv", *jh) for jh in TRANSPOSE_AFTER.get(m, [])]
        ROUND4 = len(JOBS)
        JOBS += [("norm", k, 0) for k in range(LATE_AT + 1)] + [("conv", *LATE[0])]
        JOBS += [("norm", k, 0) for k in range(LATE_AT + 1, KC)] + [("conv", *LATE[1])]
        JOBS += [("norm", k, 1) for k in range(KC)]
        NORM_BANKS = [ROUND4 % 4, (ROUND4 + 1) % 4]
        OTHERS = [(ROUND4 + 2) % 4, (ROUND4 + 3) % 4]
        BANK, USES = {}, [0] * 4
        USE = {}
        for n, job in enumerate(JOBS):
            BANK[job] = n % 4 if n < ROUND4 else NORM_BANKS[(n - ROUND4) % 2]
            USE[job] = USES[BANK[job]]
            USES[BANK[job]] += 1
        CONV_JOBS = [(j, h) for kind, j, h in JOBS if kind == "conv"]
        CT = {jh: n + 1 for n, jh in enumerate(CONV_JOBS)}
        OUTPUTS = [(t, n) for h in range(NH) for n in range(D // HALF) for t in range(TPH * h, TPH * (h + 1))]
        A, M = "acc", "mm"
        OUT_BANK = [(A, 0), (A, 2), (M, OTHERS[0]), (M, OTHERS[1]), (A, 1), (A, 3), (A, 0), (A, 2),
                    (M, OTHERS[0]), (M, OTHERS[1]), (M, NORM_BANKS[0]), (M, NORM_BANKS[1]),
                    (A, 1), (A, 3), (A, 0), (A, 2)]

        def out_bank(q):
            which, b = OUT_BANK[q]
            return (acc if which == A else mm)[:, b, :]

        def bank(job):
            return mm[:, BANK[job], :]

        def free(job):
            return bank_free[BANK[job]]

        def wait_bank(pe, job):
            if USE[job]:
                pe.wait_ge(bank_free[BANK[job]], USE[job])

        def nth(kind, m):
            return sum(k == kind for k, _ in UNITS[:m + 1])

        def gpsimd_slot(j):
            return (GPSIMD_TILES.index(j) + 1) % 2

        def columns(halves):
            return slice(HALF * halves[0], HALF * (halves[-1] + 1))

        def u_in(j, halves, k):
            return u[:, j % 4, k + HALF * halves[0]:k + HALF * (halves[-1] + 1)]

        def terms(hi1, lo1, hi2, lo2):
            return ((hi1, hi2), (hi1, lo2), (lo1, hi2))

        def half(h):
            return slice(h * HALF, (h + 1) * HALF)

        def diag(h, i):
            return sgate[:, TPH * h + i, 0:P]

        def by_pool(h, k):
            return h == 1 or k in LO_BY_POOL

        def wait_lo(engine, h, k):
            before = [(hh, kk) for hh in range(NH) for kk in range(KC) if (hh, kk) <= (h, k)]
            mine = by_pool(h, k)
            engine.wait_ge(xlo_pool if mine else xlo_ready, sum(by_pool(*hk) == mine for hk in before))

        block = ctx.enter_context(nc.Block())

        @block.sync
        def _(sp):
            def load_half(h, between):
                for t in range(TPH * h, TPH * (h + 1)):
                    sp.dma_start(sgate[:, t, :], x[t * P:(t + 1) * P, :]).then_inc(x_sq_in[t], 16)
                for k in range(KC):
                    if k in between:
                        kind, j = UNITS[between[k]]
                        sp.dma_start(raw[:, between[k], :], w_in[PART[kind], j]).then_inc(raw_in[between[k]], 16)
                    sp.dma_start(nat[:, k, half(h)], x_t[h, k]).then_inc(xt_in[h][k], 16)

            load_half(0, {0: 0, 3: 1})
            load_half(1, {})
            for m in range(2, NU):
                kind, j = UNITS[m]
                sp.wait_ge(wlo_ready, m - 1)
                sp.dma_start(raw[:, m % 2, :], w_in[PART[kind], j]).then_inc(raw_in[m % 2], 16)
            for r in range(NWO):
                m = NU + r
                sp.wait_ge(wlo_ready, m - 1)
                sp.dma_start(raw[:, m % 2, :].rearrange("p (k n) -> p k n", k=2),
                             w_out[r // (KC // 2), r % (KC // 2)]).then_inc(raw_in[m % 2], 16)
            for t in range(NT):
                sp.wait_ge(nt_ready, KC * (t // TPH + 1))
                sp.dma_start(nat[:, t, :], x[t * P:(t + 1) * P, :]).then_inc(x_in[t], 16)
            for q, (t, n) in enumerate(OUTPUTS):
                sp.wait_ge(y_added, q + 1)
                sp.dma_start(out[t * P:(t + 1) * P, n * HALF:(n + 1) * HALF],
                             nat[:, t, n * HALF:(n + 1) * HALF]).then_inc(y_out, 16)
            sp.wait_ge(y_out, 16 * NH * NT)

        @block.tensor
        def _(pe):
            def spread_rms(h):
                for i in range(TPH):
                    pe.wait_ge(diag_ready, TPH * h + i + 1)
                    ins = nc.tensor.matmul(acc[:, h, i * P:(i + 1) * P], ones[:], diag(h, i), start=True, stop=True)
                ins.then_inc(rms_all_ready, 1)

            def project_first(h):
                for m in range(2):
                    wait_bank(pe, ("unit", m, h))
                for step in range(KC + LAG):
                    if step < KC:
                        wait_lo(pe, h, step)
                    for m in range(2):
                        k = step - LAG * m
                        if not 0 <= k < KC:
                            continue
                        if k == 0:
                            pe.wait_ge(wlo_ready, m + 1)
                        for i, (w, xx) in enumerate(terms(w_hi, w_lo, x_hi, x_lo)):
                            ins = nc.tensor.matmul(bank(("unit", m, h)), w[:, m % 3, k, :], xx[:, k, half(h)],
                                                   start=(k == 0 and i == 0), stop=(k == KC - 1 and i == 2))
                        if k == KC - 1:
                            ins.then_inc(unit_ready[UNITS[m][0]], 1)
                    if h == 0 and step == SPREAD_AT:
                        spread_rms(1)

            def project(m, h):
                kind, _ = UNITS[m]
                pe.wait_ge(wlo_ready, m + 1)
                wait_bank(pe, ("unit", m, h))
                for k in range(KC):
                    for i, (w, xx) in enumerate(terms(w_hi, w_lo, x_hi, x_lo)):
                        ins = nc.tensor.matmul(bank(("unit", m, h)), w[:, m % 3, k, :],
                                               xx[:, k, h * HALF:(h + 1) * HALF],
                                               start=(k == 0 and i == 0), stop=(k == KC - 1 and i == 2))
                    if (m, h, k) == (NU - 1, 1, NORM_AT):
                        for kk in range(AHEAD):
                            transpose_norm(kk, 0)
                ins.then_inc(unit_ready[kind], 1)

            def transpose_conv(j, h):
                wait_bank(pe, ("conv", j, h))
                if (j, h) in STEP_END:
                    pe.wait_ge(steps_done, STEP_END[j, h])
                    src = dconv[:, :] if (j, h) != (6, 1) else pconv[:, gpsimd_slot(j), :]
                else:
                    pe.wait_ge(sums_done, SUM_END[j, h])
                    src = pconv[:, gpsimd_slot(j), :]
                for i in range(TPH):
                    t = TPH * h + i
                    ins = nc.tensor.transpose(bank(("conv", j, h))[:, i * P:(i + 1) * P],
                                              src[:, t * P:(t + 1) * P], ident[:])
                ins.then_inc(ct_ready, 1)

            def transpose_norm(k, h):
                wait_bank(pe, ("norm", k, h))
                pe.wait_ge(norm_dve, TPH // 2 * (h + 1))
                pe.wait_ge(norm_act, TPH // 2 * (h + 1))
                for i in range(TPH):
                    t = TPH * h + i
                    ins = nc.tensor.transpose(bank(("norm", k, h))[:, i * P:(i + 1) * P],
                                              nat[:, t, k * P:(k + 1) * P], ident[:])
                ins.then_inc(nt_ready, 1)

            def out_product(dst, t, n, k):
                for i, (v, w) in enumerate(terms(x_hi, x_lo, *wo[n, k // 2])):
                    ins = nc.tensor.matmul(dst, v[:, k, t * P:(t + 1) * P], w[:, k % 2, :],
                                           start=(k == 0 and i == 0), stop=(k == KC - 1 and i == 2))
                return ins

            pe.wait_ge(consts_in, 32)
            pe.wait_ge(ones_ready, 1)
            spread_rms(0)
            for h in range(NH):
                project_first(h)
            for m in range(2, NU):
                project(m, 0)
                project(m, 1)
                for j, h in TRANSPOSE_AFTER.get(m, []):
                    transpose_conv(j, h)

            pe.wait_ge(steps_done, STEP_END[7, 0])
            for b in OTHERS:
                pe.wait_ge(bank_free[b], USES[b])
            for k in range(KC + AHEAD):
                if AHEAD <= k < KC:
                    transpose_norm(k, 0)
                if k >= AHEAD:
                    pe.wait_ge(vlo_ready, k - AHEAD + 1)
                    pe.wait_ge(wlo_ready, NU + (k - AHEAD) // 2 + 1)
                    for q in range(TPH):
                        ins = out_product(out_bank(q), *OUTPUTS[q], k - AHEAD)
                        if k == KC + AHEAD - 1:
                            ins.then_inc(y_ready, 1)
                if k == LATE_AT:
                    transpose_conv(*LATE[0])
            transpose_conv(*LATE[1])
            for q in range(TPH, NH * NT):
                if OUT_BANK[q] in OUT_BANK[:q]:
                    before = max(i for i in range(q) if OUT_BANK[i] == OUT_BANK[q])
                    pe.wait_ge(y_added, before + 1)
                elif OUT_BANK[q][0] == M:
                    b = OUT_BANK[q][1]
                    pe.wait_ge(bank_free[b], USES[b])
                else:
                    pe.wait_ge(steps_done, len(STEPS))
                for k in range(KC):
                    if q == TPH:
                        pe.wait_ge(wlo_ready, NU + (KC + k) // 2 + 1)
                    if q == 2 * TPH:
                        pe.wait_ge(vlo_ready, KC + k + 1)
                    ins = out_product(out_bank(q), *OUTPUTS[q], k)
                    if q in (6, 7) and k % 2:
                        transpose_norm(4 * (q - 6) + k // 2, 1)
                ins.then_inc(y_ready, 1)

        @block.scalar
        def _(act):
            act.dma_start(chan[:], per_channel).then_inc(consts_in, 16)
            act.dma_start(ident[:], identity).then_inc(consts_in, 16)

            def square(t):
                act.wait_ge(x_sq_in[t], 16)
                nc.scalar.activation(sgate[:, t, :], sgate[:, t, :], ACT.Square,
                                     accum_out=mean_sq[:, t:t + 1]).then_inc(sumsq_ready, 1)

            def split_x(h, k):
                act.wait_ge(hn_ready, KC * h + k + 1)
                nc.scalar.activation(x_hi[:, k, half(h)], nat[:, k, half(h)], ACT.Copy).then_inc(xhi_ready, 1)

            def split_w(m):
                act.wait_ge(raw_in[m % 2], 16 * (m // 2 + 1))
                if m >= 3:
                    count_used(m - 3)
                nc.scalar.activation(w_hi[:, m % 3, :, :].rearrange("p k n -> p (k n)"), raw[:, m % 2, :],
                                     ACT.Copy).then_inc(whi_ready, 1)

            def count_used(m):
                kind, _ = UNITS[m]
                act.wait_ge(unit_ready[kind], NH * nth(kind, m))

            def read_unit(m, h):
                kind, j = UNITS[m]
                act.wait_ge(unit_ready[kind], NH * (nth(kind, m) - 1) + h + 1)
                if kind == "b":
                    if j >= 1:
                        act.wait_ge(u_ready, NH * (j - 1) + h + 1)
                    nc.scalar.activation(sig[:, h, :], bank(("unit", m, h)), ACT.Sigmoid).then_inc(sig_ready, 1)
                    act.wait_ge(sig_ready, NH * j + h + 1)
                    act.sem_inc(free(("unit", m, h)), 1)
                else:
                    nc.scalar.activation(sgate[:, j, h * HALF:(h + 1) * HALF], bank(("unit", m, h)),
                                         ACT.Silu).then_inc(free(("unit", m, h)), 1)

            def product(n):
                j, halves, k = PRODUCTS[n]
                if k == 0:
                    act.wait_ge(u_ready, 1 if j == 0 and halves == (0,) else NH * (j + 1))
                if n >= 3:
                    act.wait_ge(sums_done, SUM_OF[n - 3])
                nc.scalar.activation(prod[:, n % 3, 0:HALF * len(halves)], u_in(j, halves, k), ACT.Identity,
                                     scale=conv_w[:, j, k:k + 1],
                                     bias=conv_b[:, j:j + 1] if k == 0 else 0.0).then_inc(prod_ready, 1)

            def copy_conv(j, h):
                act.wait_ge(ct_ready, CT[j, h])
                nc.scalar.activation(nat[:, TPH * h:TPH * (h + 1), j * P:(j + 1) * P],
                                     bank(("conv", j, h)).rearrange("p (t c) -> p t c", c=P),
                                     ACT.Copy).then_inc(ct_copied, 1)
                act.wait_ge(ct_copied, CT[j, h])
                act.sem_inc(free(("conv", j, h)), 1)

            def split_wo(r):
                m = NU + r
                n, kp = divmod(r, KC // 2)
                act.wait_ge(raw_in[m % 2], 16 * (m // 2 + 1))
                nc.scalar.activation(wo[n, kp][0][:],
                                     raw[:, m % 2, :].rearrange("p (k n) -> p k n", k=2),
                                     ACT.Copy).then_inc(whi_ready, 1)

            def normalise(h):
                act.wait_ge(shift_ready, h + 1)
                for t in range(TPH * h + TPH // 2, TPH * (h + 1)):
                    nc.scalar.activation(nat[:, t, :], nat[:, t, :], ACT.Identity, scale=rstd[:, t:t + 1],
                                         bias=shift[:, t:t + 1]).then_inc(norm_act, 1)

            def act_norm(k, h):
                n = KC * h + k
                act.wait_ge(nt_ready, n + 1)
                if n >= 2:
                    act.wait_ge(v_ready, n - 1)
                nc.scalar.activation(sig[:, n % 2, :], bank(("norm", k, h)), ACT.Silu, scale=ln_g[:, k:k + 1],
                                     bias=ln_b[:, k:k + 1]).then_inc(actv_ready, 1)
                act.wait_ge(actv_ready, n + 1)
                act.sem_inc(free(("norm", k, h)), 1)

            def split_v(k, h):
                act.wait_ge(v_ready, KC * h + k + 1)
                part = slice(HALF * h, HALF * (h + 1))
                nc.scalar.activation(x_hi[:, k, part], sgate[:, k, part], ACT.Copy).then_inc(vhi_ready, 1)

            for t in range(TPH):
                square(t)
            split_w(0)
            for k in range(KC):
                split_x(0, k)
                if k == 1:
                    split_w(1)
                for i in range(TPH):
                    if SQUARE_AT[i] == k:
                        square(TPH + i)
            for k in range(KC):
                split_x(1, k)
                if k == SIGMOID_AT:
                    read_unit(0, 0)

            made = 0
            for m in range(NU):
                if m + 2 < NU:
                    split_w(m + 2)
                for j, h in TRANSPOSE_AFTER.get(m - 1, []):
                    copy_conv(j, h)
                quota = min(products_by[m], PRODUCT_END[6, 0] + RSTD_TAP + 4)
                middle = (made + quota) // 2
                while made < middle:
                    product(made)
                    made += 1
                if UNITS[m][0] != "a" and m > 0:
                    read_unit(m, 0)
                while made < quota:
                    product(made)
                    made += 1
                if m == NU - 1:
                    while made < PRODUCT_END[6, 0] + RSTD_TAP + 4:
                        product(made)
                        made += 1
                    normalise(0)
                    count_used(NU - 2)
                    act.wait_ge(u_ready, NH * KC)
                    split_wo(0)
                    while made < len(PRODUCTS) - STREAM_PRODUCTS:
                        product(made)
                        made += 1
                    act_norm(0, 0)
                    split_v(0, 0)
                if UNITS[m][0] != "a":
                    read_unit(m, 1)

            count_used(NU - 1)
            act.wait_ge(prod_ready, PRODUCT_END[1, 1])
            act.wait_ge(steps_done, STEP_END[5, 1])
            for k in range(KC + 1):
                if 0 < k < KC:
                    act_norm(k, 0)
                if k == LATE_AT:
                    copy_conv(*LATE[0])
                if k > 1:
                    split_v(k - 1, 0)
                if k == SPLIT_WITH[4]:
                    act.wait_ge(sums_done, SUM_OF[-1])
                if k in SPLIT_WITH.values():
                    split_wo({n: r for r, n in SPLIT_WITH.items()}[k])
                if k > 0 and made < len(PRODUCTS):
                    product(made)
                    made += 1
            assert made == len(PRODUCTS)
            copy_conv(*LATE[1])
            for r in range(6, NWO):
                split_wo(r)
            normalise(1)
            for k in range(KC + 1):
                if k < KC:
                    act_norm(k, 1)
                if k > 0:
                    split_v(k - 1, 1)

        @block.vector
        def _(dve):
            nc.vector.memset(ones[:], 1.0).then_inc(ones_ready, 1)
            nc.vector.memset(half_neg[:], -0.5).then_inc(exponent_ready, 1)
            nc.vector.memset(u[:, :, 0:PAD], 0.0).then_inc(pads_ready, 1)
            dve.wait_ge(pads_ready, 1)

            def rms_diagonal(h):
                for i in range(TPH):
                    t = TPH * h + i
                    dve.wait_ge(rms_ready, t + 1)
                    if t == 0:
                        dve.wait_ge(consts_in, 32)
                    nc.vector.tensor_scalar(diag(h, i), ident[:], rms[:, t:t + 1], None,
                                            ALU.mult).then_inc(diag_ready, 1)

            def make_hn(h, k):
                if k == 0:
                    dve.wait_ge(rms_all_ready, h + 1)
                dve.wait_ge(xt_in[h][k], 16)
                nc.vector.scalar_tensor_tensor(nat[:, k, half(h)], nat[:, k, half(h)], norm_g[:, k:k + 1],
                                               acc[:, h, :], ALU.mult, ALU.mult).then_inc(hn_ready, 1)

            def split_x(h, k):
                dve.wait_ge(xhi_ready, KC * h + k + 1)
                nc.vector.tensor_tensor(x_lo[:, k, half(h)], nat[:, k, half(h)], x_hi[:, k, half(h)].bitcast(F32),
                                        ALU.subtract).then_inc(xlo_ready, 1)

            def split_w(m):
                if m == 2:
                    dve.wait_ge(wlo_ready, 2)
                dve.wait_ge(whi_ready, m + 1)
                nc.vector.tensor_tensor(w_lo[:, m % 3, :, :].rearrange("p k n -> p (k n)"), raw[:, m % 2, :],
                                        w_hi[:, m % 3, :, :].rearrange("p k n -> p (k n)").bitcast(F32),
                                        ALU.subtract).then_inc(wlo_ready, 1)

            def conv_in(m, h):
                _, j = UNITS[m]
                dve.wait_ge(unit_ready["a"], NH * j + h + 1)
                dve.wait_ge(sig_ready, NH * j + h + 1)
                if j >= 4:
                    if (j - 4, 1) in STEP_END:
                        dve.wait_ge(steps_done, STEP_END[j - 4, 1])
                    if (j - 4, 1) in PRODUCT_END:
                        dve.wait_ge(prod_ready, PRODUCT_END[j - 4, 1])
                nc.vector.tensor_tensor(u[:, j % 4, PAD + h * HALF:PAD + (h + 1) * HALF], bank(("unit", m, h)),
                                        sig[:, h, :], ALU.mult).then_inc(u_ready, 1)
                dve.wait_ge(u_ready, NH * j + h + 1)
                dve.sem_inc(free(("unit", m, h)), 1)

            def step(n):
                j, halves, k = STEPS[n]
                cols = columns(halves)
                even, odd = (acc[:, b + halves[0]:b + halves[-1] + 1, :].rearrange("p a b -> p (a b)")
                             for b in (0, 2))
                if k in ("even", "odd"):
                    dve.wait_ge(steps_done, n)
                    dve.wait_ge(sums_done, SUM_END[j, 1])
                    both = pconv[:, gpsimd_slot(j), cols]
                    nc.vector.tensor_tensor(both, even if k == "even" else odd, both, ALU.add).then_inc(steps_done, 1)
                    return
                if k in ("join", "gpsimd"):
                    dve.wait_ge(steps_done, n)
                    other = even
                    if k == "gpsimd":
                        dve.wait_ge(sums_done, SUM_END[j, 1])
                        other = pconv[:, gpsimd_slot(j), cols]
                    nc.vector.tensor_tensor(dconv[:, cols], other, dconv[:, cols], ALU.add).then_inc(steps_done, 1)
                    return
                begin = FIRST_TAP[j, halves[0]]
                if k == begin:
                    dve.wait_ge(u_ready, 1 if j == 0 and halves == (0,) else NH * (j + 1))
                if n == 0:
                    dve.wait_ge(hn_ready, NH * KC)
                if n >= 2:
                    dve.wait_ge(steps_done, n if k == begin else n - 1)
                w = conv_w[:, j, k:k + 1]
                dst = odd if k % 2 else even
                if k == 0:
                    ins = nc.vector.tensor_scalar(dst, u_in(j, halves, k), w, conv_b[:, j:j + 1], ALU.mult, ALU.add)
                elif k < begin + 2:
                    ins = nc.vector.tensor_scalar(dst, u_in(j, halves, k), w, None, ALU.mult)
                else:
                    running = dst
                    if k == TAPS - 2 and (j, halves) != (6, (1,)):
                        dst = dconv[:, cols]
                        before = VECTOR_TILES[:VECTOR_TILES.index(j)]
                        if before:
                            dve.wait_ge(ct_ready, CT[before[-1], halves[-1]])
                    ins = nc.vector.scalar_tensor_tensor(dst, u_in(j, halves, k), w, running, ALU.mult, ALU.add)
                ins.then_inc(steps_done, 1)

            def split_wo(r):
                m = NU + r
                n, kp = divmod(r, KC // 2)
                dve.wait_ge(whi_ready, m + 1)
                hi, lo = wo[n, kp]
                nc.vector.tensor_tensor(lo[:], raw[:, m % 2, :].rearrange("p (k n) -> p k n", k=2), hi[:].bitcast(F32),
                                        ALU.subtract).then_inc(wlo_ready, 1)

            def take_stats(g, tiles=range(NT)):
                need = max(CT[j, tiles[-1] // TPH] for j in (2 * g, 2 * g + 1))
                dve.wait_ge(ct_copied, need)
                for t in tiles:
                    nc.vector.bn_stats(stats[:, t, g, :], nat[:, t, 2 * g * P:2 * (g + 1) * P]).then_inc(stats_ready, 1)

            def moments(h):
                tiles = range(TPH * h, TPH * (h + 1))
                take_stats(KC // 2 - 1, tiles)
                dve.wait_ge(stats_ready, NT * (KC // 2 - 1) + TPH * (h + 1))
                for t in tiles:
                    nc.vector.bn_aggr(mean_var[:, t, :],
                                      stats[:, t, :, :].rearrange("p g s -> p (g s)")).then_inc(mv_ready, 1)

            def normalise(h):
                dve.wait_ge(rstd_ready, h + 1)
                part = slice(TPH * h, TPH * (h + 1))
                nc.vector.scalar_tensor_tensor(shift[:, part], mean_var[:, part, 0], -1.0, rstd[:, part], ALU.mult,
                                               ALU.mult).then_inc(shift_ready, 1)
                for t in range(TPH * h, TPH * h + TPH // 2):
                    nc.vector.tensor_scalar(nat[:, t, :], nat[:, t, :], mean_var[:, t, 0:1], rstd[:, t:t + 1],
                                            ALU.subtract, ALU.mult).then_inc(norm_dve, 1)

            def gate(k, h):
                n = KC * h + k
                part = slice(h * HALF, (h + 1) * HALF)
                dve.wait_ge(actv_ready, n + 1)
                job = ("unit", UNITS.index(("g", k)), h)
                dve.wait_ge(free(job), USE[job] + 1)
                nc.vector.tensor_tensor(sgate[:, k, part], sig[:, n % 2, :], sgate[:, k, part],
                                        ALU.mult).then_inc(v_ready, 1)

            def split_v(k, h):
                part = slice(h * HALF, (h + 1) * HALF)
                dve.wait_ge(vhi_ready, KC * h + k + 1)
                nc.vector.tensor_tensor(x_lo[:, k, part], sgate[:, k, part], x_hi[:, k, part].bitcast(F32),
                                        ALU.subtract).then_inc(vlo_ready, 1)

            def add_x(q):
                t, n = OUTPUTS[q]
                dve.wait_ge(x_in[t], 16)
                dve.wait_ge(y_ready, q + 1)
                part = (slice(None), t, slice(n * HALF, (n + 1) * HALF))
                nc.vector.tensor_tensor(nat[part], out_bank(q), nat[part], ALU.add).then_inc(y_added, 1)

            rms_diagonal(0)
            split_w(0)
            make_hn(0, 0)
            for k in range(KC):
                if k + 1 < KC:
                    make_hn(0, k + 1)
                if not by_pool(0, k):
                    split_x(0, k)
                if k == DIAG_AT:
                    rms_diagonal(1)
            for k in range(KC):
                make_hn(1, k)
                if k == CONV_IN_AT:
                    conv_in(1, 0)

            total = len(STEPS)
            done = 0
            for m in range(NU):
                if m + 2 < NU:
                    split_w(m + 2)
                quota = min(steps_by[m], total - 2)
                middle = (done + quota) // 2
                if m == NU - 1:
                    middle = quota = done + STEPS_BEFORE_MOMENTS
                if m > 0 and UNITS[m - 1][0] == "a":
                    if done < quota and UNITS.index(("a", STEPS[done][0])) < m - 1:
                        step(done)
                        done += 1
                    conv_in(m - 1, 1)
                while done < middle:
                    step(done)
                    done += 1
                if UNITS[m][0] == "a" and m > 1:
                    conv_in(m, 0)
                while done < quota:
                    step(done)
                    done += 1
                for g in STATS_AFTER.get(m, []):
                    take_stats(g)
                if m == NU - 1:
                    moments(0)
                    for _ in range(STEPS_BEFORE_NORM):
                        step(done)
                        done += 1
                    normalise(0)
                    for _ in range(STEPS_AFTER_NORM):
                        step(done)
                        done += 1
                    gate(0, 0)
                    split_wo(0)
                    split_v(0, 0)
            for k in range(KC + 1):
                if 0 < k < KC:
                    gate(k, 0)
                if k > 1:
                    split_v(k - 1, 0)
                if k in SPLIT_WITH.values():
                    split_wo({n: r for r, n in SPLIT_WITH.items()}[k])
                for _ in range(STREAM_STEPS):
                    if k > 0 and done < total:
                        step(done)
                        done += 1
            assert done == total
            moments(1)
            for r in range(6, NWO):
                split_wo(r)
            normalise(1)
            for q in range(6):
                add_x(q)
            for k in range(KC + 1):
                if k < KC:
                    gate(k, 1)
                if k > 0:
                    split_v(k - 1, 1)
                if k == 4:
                    add_x(6)
            for q in range(7, NH * NT):
                add_x(q)

        @block.gpsimd
        def _(pool):
            def inverse_deviation(h):
                part = slice(TPH * h, TPH * (h + 1))
                pool.wait_ge(mv_ready, TPH * (h + 1))
                nc.gpsimd.tensor_scalar(var_eps[:, part], mean_var[:, part, 1], 1.0, LN_EPS, ALU.mult,
                                        ALU.add).then_inc(veps_ready, 1)
                pool.wait_ge(veps_ready, h + 1)
                nc.gpsimd.tensor_tensor(rstd[:, part], var_eps[:, part], half_neg[:, part],
                                        ALU.pow).then_inc(rstd_ready, 1)

            def inverse_rms(t):
                part = slice(t, t + 1)
                pool.wait_ge(sumsq_ready, t + 1)
                nc.gpsimd.tensor_scalar(mean_sq[:, part], mean_sq[:, part], 1.0 / D, RMS_EPS, ALU.mult,
                                        ALU.add).then_inc(ms_ready, 1)
                pool.wait_ge(ms_ready, t + 1)
                nc.gpsimd.tensor_tensor(rms[:, part], mean_sq[:, part], half_neg[:, part],
                                        ALU.pow).then_inc(rms_ready, 1)

            pool.wait_ge(exponent_ready, 1)
            for t in range(TPH):
                inverse_rms(t)
            pool.wait_ge(whi_ready, 2)
            pool.wait_ge(wlo_ready, 1)
            nc.gpsimd.tensor_tensor(w_lo[:, 1, :, :].rearrange("p k n -> p (k n)"), raw[:, 1, :],
                                    w_hi[:, 1, :, :].rearrange("p k n -> p (k n)").bitcast(F32),
                                    ALU.subtract).then_inc(wlo_ready, 1)
            t = TPH
            for h in range(NH):
                for k in range(KC):
                    while h == 0 and t < NT and POW_AT[t - TPH] == k:
                        inverse_rms(t)
                        t += 1
                    if by_pool(h, k):
                        pool.wait_ge(xhi_ready, KC * h + k + 1)
                        nc.gpsimd.tensor_tensor(x_lo[:, k, half(h)], nat[:, k, half(h)],
                                                x_hi[:, k, half(h)].bitcast(F32), ALU.subtract).then_inc(xlo_pool, 1)

            n, p = 0, 0
            for j, halves, taps in GPSIMD_PARTS:
                dst = pconv[:, gpsimd_slot(j), columns(halves)]
                i = GPSIMD_TILES.index(j)
                if i >= 2:
                    held = (GPSIMD_TILES[i - 2], halves[-1])
                    if held in STEP_END:
                        pool.wait_ge(steps_done, STEP_END[held])
                    else:
                        pool.wait_ge(ct_ready, CT[held])
                for k in taps:
                    if k > 0:
                        pool.wait_ge(prod_ready, p + 1)
                        if k > 1:
                            pool.wait_ge(sums_done, n)
                        width = slice(0, HALF * len(halves))
                        nc.gpsimd.tensor_tensor(dst, prod[:, (p - 1) % 3, width] if k == 1 else dst,
                                                prod[:, p % 3, width], ALU.add).then_inc(sums_done, 1)
                        n += 1
                    p += 1
                    if (j, halves, k) == (6, (1,), RSTD_TAP):
                        inverse_deviation(0)
            inverse_deviation(1)


def kernel(**inputs):
    import numpy as np
    import concourse.bacc as bacc
    from concourse.bass_utils import run_bass_kernel_spmd

    def arr(name):
        return np.asarray(inputs[name])

    x = arr("x")[0]
    T, D = x.shape
    KC = D // P
    x_t = x.T.reshape(KC, P, T // HALF, HALF).transpose(2, 0, 1, 3)
    w_in, w_out = arr("a_w_in")[0], arr("a_w_out")[0]
    conv_w = arr("a_conv_w")[0]
    w_in = w_in.reshape(KC, P, 3, KC, P).transpose(2, 3, 1, 0, 4).reshape(3, KC, P, KC * P)
    w_out = w_out.reshape(KC // 2, 2, P, D // HALF, HALF).transpose(3, 0, 2, 1, 4)

    def by_channel(v):
        return v.reshape(KC, P).T

    per_channel = np.concatenate(
        [conv_w.reshape(-1, KC, P).transpose(2, 1, 0).reshape(P, -1)]
        + [by_channel(arr(n)[0]) for n in ("a_conv_b", "a_ln_g", "a_ln_b", "norm_g")], axis=1)
    arrays = {k: np.ascontiguousarray(v) for k, v in {
        "x": x, "x_t": x_t, "w_in": w_in, "w_out": w_out, "per_channel": per_channel,
        "identity": np.eye(P, dtype=np.float32)}.items()}

    nc = bacc.Bacc("TRN2", target_bir_lowering=False, num_devices=1)
    aps = [nc.dram_tensor(k, v.shape, F32, kind="ExternalInput").ap() for k, v in arrays.items()]
    out = nc.dram_tensor("y", [T, D], F32, kind="ExternalOutput").ap()
    gated_conv_layer(nc, *aps, out)
    r = run_bass_kernel_spmd(nc, [arrays], core_ids=[0])
    return r.results[0]["y"].reshape(1, T, D)
```
